# Optimizing a Trainium2 kernel written in Bass

```python
import math
import jax
import jax.numpy as jnp
from jax import lax
import numpy as np

D_MODEL = 1024
BATCH = 1
SEQ = 512
DEPTH = 1

GRID_W = 64
CTX_LEN = 256
N_MIXERS = 4
NORM_EPS = 1e-6
ROPE_BASE = 10000.0

GDN_DK = 128
GDN_DV = 128
GDN_HEADS = D_MODEL // GDN_DV
GDN_CONV = 5
GDN_CHUNK = 64
GDN_PROJ = 2 * GDN_HEADS * GDN_DK + 2 * GDN_HEADS * GDN_DV + 4 * GDN_HEADS

MLSTM_DV = 128
MLSTM_DQK = MLSTM_DV // 2
MLSTM_HEADS = D_MODEL // MLSTM_DV
MLSTM_CHUNK = 64
MLSTM_PROJ = 2 * MLSTM_HEADS * MLSTM_DQK + 2 * MLSTM_HEADS * MLSTM_DV + 4 * MLSTM_HEADS

DIFF_DH = 64
DIFF_HEADS = D_MODEL // (2 * DIFF_DH)
DIFF_PROJ = 6 * DIFF_HEADS * DIFF_DH

SWA_DH = 64
SWA_QHEADS = D_MODEL // SWA_DH
SWA_KVHEADS = SWA_QHEADS // 4
SWA_WINDOW = 128
SWA_PROJ = (SWA_QHEADS + 2 * SWA_KVHEADS) * SWA_DH

ATTN_QBLOCK = 128

N_EXPERTS = 32
TOP_K = 4
D_FF = D_MODEL
SWIGLU_ALPHA = 1.702
SWIGLU_LIMIT = 7.0
MOE_BLOCK = 128

kernel_name = 'hybrid_interleaved_dit_moe_trunk'

def _layers_using(m):
    return len(range(m, DEPTH, N_MIXERS))

def _rmsnorm(x, g):
    xf = x.astype(jnp.float32)
    y = xf * lax.rsqrt(jnp.mean(xf * xf, axis=-1, keepdims=True) + NORM_EPS)
    return (y * g.astype(jnp.float32)).astype(x.dtype)

def _modulate(h, shift, scale):
    return h * (1 + scale) + shift

def _l2norm(t):
    tf = t.astype(jnp.float32)
    return tf * lax.rsqrt(jnp.sum(tf * tf, axis=-1, keepdims=True) + NORM_EPS)

def _heads(t, n):
    b, l, _ = t.shape
    return t.reshape(b, l, n, -1).transpose(0, 2, 1, 3)

def _axial_rope_tables(seq, head_dim):
    rows = seq // GRID_W
    row = jnp.repeat(jnp.arange(rows), GRID_W).astype(jnp.float32)
    col = jnp.tile(jnp.arange(GRID_W), rows).astype(jnp.float32)
    quarter = head_dim // 4
    inv = ROPE_BASE ** (-jnp.arange(quarter, dtype=jnp.float32) / quarter)
    ang_r = row[:, None] * inv[None, :]
    ang_c = col[:, None] * inv[None, :]
    return (jnp.cos(ang_r), jnp.sin(ang_r), jnp.cos(ang_c), jnp.sin(ang_c))

def _apply_axial_rope(t, tables):
    cr, sr, cc, sc = tables
    q = cr.shape[-1]
    tf = t.astype(jnp.float32)

    def rot(seg, cos, sin):
        a, b = seg[..., :q], seg[..., q:]
        return jnp.concatenate([a * cos - b * sin, b * cos + a * sin], axis=-1)

    out = jnp.concatenate([rot(tf[..., :2 * q], cr, sr), rot(tf[..., 2 * q:], cc, sc)], axis=-1)
    return out.astype(t.dtype)

def _centred_dwconv(t, w):
    k, ch = w.shape
    return lax.conv_general_dilated(t, w[:, None, :].astype(t.dtype), window_strides=(1,),
                                    padding=[(k // 2, k // 2)], dimension_numbers=('NWC', 'WIO', 'NWC'),
                                    feature_group_count=ch)

def _flip(t):
    return jnp.flip(t, axis=2)

def _bidirectional_prefix_scan(scan_fn, ctx_f, ctx_b, lat_f, lat_b, state0):
    oc_f, st_f = scan_fn(*ctx_f, state0)
    ox_f, _ = scan_fn(*lat_f, st_f)
    oc_b, st_b = scan_fn(*[_flip(t) for t in ctx_b], state0)
    ox_b, _ = scan_fn(*[_flip(t) for t in lat_b], st_b)
    return oc_f + _flip(oc_b), ox_f + _flip(ox_b)

def _gated_delta_chunked(q, k, v, beta, g, state):
    B, H, L, dk = q.shape
    dv = v.shape[-1]
    C = GDN_CHUNK
    n = L // C
    q = (q.astype(jnp.float32) * dk ** -0.5).reshape(B, H, n, C, dk)
    k = k.astype(jnp.float32).reshape(B, H, n, C, dk)
    v = v.astype(jnp.float32).reshape(B, H, n, C, dv)
    beta = beta.reshape(B, H, n, C)
    g = jnp.cumsum(g.reshape(B, H, n, C), axis=-1)
    tri = jnp.tril(jnp.ones((C, C), bool))
    stri = jnp.tril(jnp.ones((C, C), bool), -1)
    gam = jnp.exp(jnp.where(tri, g[..., :, None] - g[..., None, :], -jnp.inf))
    kb = k * beta[..., None]
    a_low = jnp.where(stri, jnp.einsum('bhnid,bhnjd->bhnij', kb, k) * gam, 0.0)
    rhs = jnp.concatenate([v * beta[..., None], kb * jnp.exp(g)[..., None]], axis=-1)
    sol = lax.linalg.triangular_solve(jnp.eye(C, dtype=jnp.float32) + a_low, rhs, left_side=True,
                                      lower=True, unit_diagonal=True)
    u, w = sol[..., :dv], sol[..., dv:]
    qk = jnp.einsum('bhnid,bhnjd->bhnij', q, k) * gam
    qg = q * jnp.exp(g)[..., None]
    kd = k * jnp.exp(g[..., -1:] - g)[..., None]
    g_end = jnp.exp(g[..., -1])

    def step(s, inp):
        u_c, w_c, qg_c, qk_c, kd_c, ge_c = inp
        v_new = u_c - jnp.einsum('bhck,bhkv->bhcv', w_c, s)
        o = jnp.einsum('bhck,bhkv->bhcv', qg_c, s) + jnp.einsum('bhcs,bhsv->bhcv', qk_c, v_new)
        s = s * ge_c[..., None, None] + jnp.einsum('bhck,bhcv->bhkv', kd_c, v_new)
        return s, o

    xs = tuple(jnp.moveaxis(t, 2, 0) for t in (u, w, qg, qk, kd, g_end))
    s_fin, o = lax.scan(step, state, xs)
    return jnp.moveaxis(o, 0, 2).reshape(B, H, L, dv), s_fin

def _mlstm_chunked(q, k, v, logi, logf, state):
    B, H, L, dqk = q.shape
    dv = v.shape[-1]
    C = MLSTM_CHUNK
    n = L // C
    q = q.astype(jnp.float32).reshape(B, H, n, C, dqk)
    k = (k.astype(jnp.float32) * dqk ** -0.5).reshape(B, H, n, C, dqk)
    v = v.astype(jnp.float32).reshape(B, H, n, C, dv)
    logi = logi.reshape(B, H, n, C)
    b = jnp.cumsum(logf.reshape(B, H, n, C), axis=-1)
    tri = jnp.tril(jnp.ones((C, C), bool))
    dlog = jnp.where(tri, b[..., :, None] - b[..., None, :] + logi[..., None, :], -jnp.inf)
    m_intra = jnp.max(dlog, axis=-1)
    b_last = b[..., -1]
    a_loc = b_last[..., None] - b + logi
    m_loc = jnp.max(a_loc, axis=-1)
    w_loc = jnp.exp(a_loc - m_loc[..., None])
    c_loc = jnp.einsum('bhnc,bhncv,bhnck->bhnvk', w_loc, v, k)
    n_loc = jnp.einsum('bhnc,bhnck->bhnk', w_loc, k)

    def step(carry, inp):
        c_st, n_st, m_st = carry
        cl, nl, ml, bl = inp
        m_new = jnp.maximum(bl + m_st, ml)
        sp = jnp.exp(bl + m_st - m_new)
        sl = jnp.exp(ml - m_new)
        new = (c_st * sp[..., None, None] + cl * sl[..., None, None], n_st * sp[..., None] + nl * sl[..., None], m_new)
        return new, (c_st, n_st, m_st)

    xs = tuple(jnp.moveaxis(t, 2, 0) for t in (c_loc, n_loc, m_loc, b_last))
    final, (c_in, n_in, m_in) = lax.scan(step, state, xs)
    c_in = jnp.moveaxis(c_in, 0, 2)
    n_in = jnp.moveaxis(n_in, 0, 2)
    m_in = jnp.moveaxis(m_in, 0, 2)
    log_inter = b + m_in[..., None]
    m_t = jnp.maximum(log_inter, m_intra)
    w_inter = jnp.exp(log_inter - m_t)
    pm = jnp.exp(dlog - m_t[..., None]) * jnp.einsum('bhntd,bhnsd->bhnts', q, k)
    num = w_inter[..., None] * jnp.einsum('bhntd,bhnvd->bhntv', q, c_in) + jnp.einsum('bhnts,bhnsv->bhntv', pm, v)
    den = w_inter * jnp.einsum('bhntd,bhnd->bhnt', q, n_in) + jnp.sum(pm, axis=-1)
    h = num / jnp.maximum(jnp.abs(den), jnp.exp(-m_t))[..., None]
    return h.reshape(B, H, L, dv), final

def _gdn_mixer(hc, hx, w_in, conv_w, a_log, dt_bias, norm_g, w_out, ctx_out):
    H, dk, dv = GDN_HEADS, GDN_DK, GDN_DV
    n_qk, n_v = H * dk, H * dv
    o_z = 2 * n_qk + n_v
    o_a = o_z + n_v
    a_decay = jnp.exp(a_log.astype(jnp.float32))
    dtb = dt_bias.astype(jnp.float32)

    def project(h):
        b, l, _ = h.shape
        p = h @ w_in
        qkv = jax.nn.silu(_centred_dwconv(p[..., :o_z], conv_w))
        q = _l2norm(_heads(qkv[..., :n_qk], H))
        k = _l2norm(_heads(qkv[..., n_qk:2 * n_qk], H))
        v = _heads(qkv[..., 2 * n_qk:], H)
        z = p[..., o_z:o_a].reshape(b, l, H, dv)
        ga = p[..., o_a:o_a + 2 * H].reshape(b, l, 2, H).astype(jnp.float32)
        gb = p[..., o_a + 2 * H:].reshape(b, l, 2, H).astype(jnp.float32)
        g = (-a_decay * jax.nn.softplus(ga + dtb)).transpose(2, 0, 3, 1)
        beta = jax.nn.sigmoid(gb).transpose(2, 0, 3, 1)
        return q, k, v, z, beta, g

    qc, kc, vc, zc, bc, gc = project(hc)
    qx, kx, vx, zx, bx, gx = project(hx)
    s0 = jnp.zeros((hx.shape[0], H, dk, dv), jnp.float32)
    oc, ox = _bidirectional_prefix_scan(_gated_delta_chunked,
                                        (qc, kc, vc, bc[0], gc[0]), (qc, kc, vc, bc[1], gc[1]),
                                        (qx, kx, vx, bx[0], gx[0]), (qx, kx, vx, bx[1], gx[1]), s0)

    def out(o, z, dtype):
        b, _, l, _ = o.shape
        o = _rmsnorm(o.transpose(0, 2, 1, 3).astype(dtype), norm_g) * jax.nn.silu(z)
        return o.reshape(b, l, H * dv) @ w_out

    yx = out(ox, zx, hx.dtype)
    yc = out(oc, zc, hc.dtype) if ctx_out else None
    return yc, yx

def _mlstm_mixer(hc, hx, w_in, b_i, b_f, norm_g, w_out, ctx_out):
    H, dqk, dv = MLSTM_HEADS, MLSTM_DQK, MLSTM_DV
    o1 = H * dqk
    o2 = 2 * o1
    o3 = o2 + H * dv
    o4 = o3 + H * dv
    bi = b_i.astype(jnp.float32)
    bf = b_f.astype(jnp.float32)

    def project(h):
        b, l, _ = h.shape
        p = h @ w_in
        q = _heads(p[..., :o1], H)
        k = _heads(p[..., o1:o2], H)
        v = _heads(p[..., o2:o3], H)
        og = p[..., o3:o4].reshape(b, l, H, dv)
        gi = p[..., o4:o4 + 2 * H].reshape(b, l, 2, H).astype(jnp.float32) + bi
        gf = p[..., o4 + 2 * H:].reshape(b, l, 2, H).astype(jnp.float32) + bf
        logi = gi.transpose(2, 0, 3, 1)
        logf = jax.nn.log_sigmoid(gf).transpose(2, 0, 3, 1)
        return q, k, v, og, logi, logf

    qc, kc, vc, oc_g, ic, fc = project(hc)
    qx, kx, vx, ox_g, ix, fx = project(hx)
    bsz = hx.shape[0]
    st0 = (jnp.zeros((bsz, H, dv, dqk), jnp.float32), jnp.zeros((bsz, H, dqk), jnp.float32),
           jnp.zeros((bsz, H), jnp.float32))
    hc_s, hx_s = _bidirectional_prefix_scan(_mlstm_chunked,
                                            (qc, kc, vc, ic[0], fc[0]), (qc, kc, vc, ic[1], fc[1]),
                                            (qx, kx, vx, ix[0], fx[0]), (qx, kx, vx, ix[1], fx[1]), st0)

    def out(hs, og, dtype):
        b, _, l, _ = hs.shape
        hs = _rmsnorm(hs.transpose(0, 2, 1, 3).astype(dtype), norm_g) * jax.nn.sigmoid(og)
        return hs.reshape(b, l, H * dv) @ w_out

    yx = out(hx_s, ox_g, hx.dtype)
    yc = out(hc_s, oc_g, hc.dtype) if ctx_out else None
    return yc, yx

def _diff_mixer(hc, hx, w_in, lam_p, norm_g, w_out, rope, lambda_init, ctx_out):
    H, dh, QB = DIFF_HEADS, DIFF_DH, ATTN_QBLOCK
    scale = dh ** -0.5
    lp = lam_p.astype(jnp.float32)
    lam = jnp.exp(jnp.sum(lp[0] * lp[1])) - jnp.exp(jnp.sum(lp[2] * lp[3])) + lambda_init

    def project(h):
        b, l, _ = h.shape
        p = h @ w_in
        q = p[..., :2 * H * dh].reshape(b, l, 2 * H, dh).transpose(0, 2, 1, 3)
        k = p[..., 2 * H * dh:4 * H * dh].reshape(b, l, 2 * H, dh).transpose(0, 2, 1, 3)
        v = p[..., 4 * H * dh:].reshape(b, l, H, 2 * dh).transpose(0, 2, 1, 3)
        return q, k, v

    def attend(q, k, v):
        s = jnp.einsum('bhqd,bhkd->bhqk', q, k).astype(jnp.float32) * scale
        p = jax.nn.softmax(s, axis=-1)
        p = p.reshape(p.shape[0], H, 2, p.shape[2], p.shape[3])
        a = p[:, :, 0] - lam * p[:, :, 1]
        return jnp.einsum('bhqk,bhkv->bhqv', a.astype(v.dtype), v)

    qc, kc, vc = project(hc)
    qx, kx, vx = project(hx)
    qx = _apply_axial_rope(qx, rope)
    kx = _apply_axial_rope(kx, rope)
    B, _, L, _ = qx.shape
    nb = L // QB
    k_all = jnp.concatenate([kc, kx], axis=2)
    v_all = jnp.concatenate([vc, vx], axis=2)
    q_blocks = qx.reshape(B, 2 * H, nb, QB, dh).transpose(2, 0, 1, 3, 4)
    ox = lax.map(lambda qb: attend(qb, k_all, v_all), q_blocks)
    ox = ox.transpose(1, 0, 3, 2, 4).reshape(B, L, H, 2 * dh)

    def out(o):
        b, l = o.shape[0], o.shape[1]
        o = _rmsnorm(o, norm_g) * (1.0 - lambda_init)
        return o.reshape(b, l, H * 2 * dh) @ w_out

    yx = out(ox)
    yc = out(attend(qc, kc, vc).transpose(0, 2, 1, 3)) if ctx_out else None
    return yc, yx

def _sink_softmax(s, sink_b):
    m = jnp.maximum(jnp.max(s, axis=-1, keepdims=True), sink_b)
    e = jnp.exp(s - m)
    return e / (jnp.sum(e, axis=-1, keepdims=True) + jnp.exp(sink_b - m))

def _swa_mixer(hc, hx, w_in, sink, w_out, rope, ctx_out):
    Hq, Hk, dh, W, QB = SWA_QHEADS, SWA_KVHEADS, SWA_DH, SWA_WINDOW, ATTN_QBLOCK
    G = Hq // Hk
    scale = dh ** -0.5
    sink_b = sink.astype(jnp.float32).reshape(1, Hk, G, 1, 1)

    def project(h):
        b, l, _ = h.shape
        p = h @ w_in
        q = p[..., :Hq * dh].reshape(b, l, Hq, dh).transpose(0, 2, 1, 3)
        k = p[..., Hq * dh:(Hq + Hk) * dh].reshape(b, l, Hk, dh).transpose(0, 2, 1, 3)
        v = p[..., (Hq + Hk) * dh:].reshape(b, l, Hk, dh).transpose(0, 2, 1, 3)
        return q, k, v

    qc, kc, vc = project(hc)
    qx, kx, vx = project(hx)
    qx = _apply_axial_rope(qx, rope)
    kx = _apply_axial_rope(kx, rope)
    B, _, L, _ = qx.shape
    Lc = kc.shape[2]
    qg = qx.reshape(B, Hk, G, L, dh)
    kp = jnp.pad(kx, ((0, 0), (0, 0), (W, W), (0, 0)))
    vp = jnp.pad(vx, ((0, 0), (0, 0), (W, W), (0, 0)))
    span = QB + 2 * W

    def block(jb):
        start = jb * QB
        qb = lax.dynamic_slice_in_dim(qg, start, QB, axis=3)
        kb = lax.dynamic_slice_in_dim(kp, start, span, axis=2)
        vb = lax.dynamic_slice_in_dim(vp, start, span, axis=2)
        q_pos = start + jnp.arange(QB)
        k_pos = start - W + jnp.arange(span)
        valid = (jnp.abs(q_pos[:, None] - k_pos[None, :]) <= W) & (k_pos >= 0) & (k_pos < L)
        s_loc = jnp.einsum('bkgqd,bksd->bkgqs', qb, kb).astype(jnp.float32) * scale
        s_loc = jnp.where(valid, s_loc, -jnp.inf)
        s_ctx = jnp.einsum('bkgqd,bksd->bkgqs', qb, kc).astype(jnp.float32) * scale
        probs = _sink_softmax(jnp.concatenate([s_ctx, s_loc], axis=-1), sink_b)
        return jnp.einsum('bkgqs,bksd->bkgqd', probs.astype(vb.dtype), jnp.concatenate([vc, vb], axis=2))

    ox = lax.map(block, jnp.arange(L // QB))
    yx = ox.transpose(1, 0, 4, 2, 3, 5).reshape(B, L, Hq * dh) @ w_out
    yc = None
    if ctx_out:
        qcg = qc.reshape(B, Hk, G, Lc, dh)
        s = jnp.einsum('bkgqd,bksd->bkgqs', qcg, kc).astype(jnp.float32) * scale
        oc = jnp.einsum('bkgqs,bksd->bkgqd', _sink_softmax(s, sink_b).astype(vc.dtype), vc)
        yc = oc.transpose(0, 3, 1, 2, 4).reshape(B, Lc, Hq * dh) @ w_out
    return yc, yx

def _moe(h, router_w, router_b, w_gu, b_gu, w_down, b_down):
    n, d = h.shape
    E, K, BLK = N_EXPERTS, TOP_K, MOE_BLOCK
    f = w_down.shape[1]
    logits = (h @ router_w).astype(jnp.float32) + router_b.astype(jnp.float32)
    top_v, top_i = lax.top_k(logits, K)
    gates = jax.nn.softmax(top_v, axis=-1)
    n_assign = n * K
    e_flat = top_i.reshape(-1)
    tok_flat = jnp.repeat(jnp.arange(n, dtype=jnp.int32), K)
    g_flat = gates.reshape(-1)
    order = jnp.argsort(e_flat)
    e_s, tok_s, g_s = e_flat[order], tok_flat[order], g_flat[order]
    counts = jnp.bincount(e_flat, length=E)
    starts = jnp.cumsum(counts) - counts
    padded = (counts + BLK - 1) // BLK * BLK
    pad_end = jnp.cumsum(padded)
    pad_start = pad_end - padded
    dest = pad_start[e_s] + (jnp.arange(n_assign) - starts[e_s])
    n_blk = (n_assign + BLK - 1) // BLK + E
    buf_tok = jnp.full((n_blk * BLK,), n, jnp.int32).at[dest].set(tok_s)
    buf_gate = jnp.zeros((n_blk * BLK,), jnp.float32).at[dest].set(g_s)
    blk_exp = jnp.minimum(jnp.searchsorted(pad_end, jnp.arange(n_blk) * BLK, side='right'), E - 1)
    h_pad = jnp.concatenate([h, jnp.zeros((1, d), h.dtype)], axis=0)

    def expert_block(args):
        toks, e = args
        xb = h_pad[toks]
        gu = (xb @ w_gu[e]).astype(jnp.float32) + b_gu[e].astype(jnp.float32)
        x_glu = jnp.minimum(gu[:, :f], SWIGLU_LIMIT)
        x_lin = jnp.clip(gu[:, f:], -SWIGLU_LIMIT, SWIGLU_LIMIT)
        act = (x_glu * jax.nn.sigmoid(SWIGLU_ALPHA * x_glu) * (x_lin + 1.0)).astype(h.dtype)
        return act @ w_down[e] + b_down[e]

    y = lax.map(expert_block, (buf_tok.reshape(n_blk, BLK), blk_exp))
    y = (y.reshape(-1, d).astype(jnp.float32) * buf_gate[:, None]).astype(h.dtype)
    return jnp.zeros((n + 1, d), h.dtype).at[buf_tok].add(y)[:n]

def setup_inputs(seed: int = 0) -> dict:
    key = jax.random.key(seed)
    ks = iter(jax.random.split(key, 48))
    D = D_MODEL

    def nrm(shape, scale):
        return jax.random.normal(next(ks), shape, jnp.float32) * scale

    nA, nB, nC, nD = [_layers_using(m) for m in range(N_MIXERS)]
    x = nrm((BATCH, SEQ, D), 1.0)
    c = nrm((BATCH, D), 1.0)
    ctx = nrm((BATCH, CTX_LEN, D), 1.0)
    c_ctx = nrm((D,), 1.0)
    ada_w = nrm((DEPTH, D, 6 * D), 0.5 * D ** -0.5)
    ada_b = nrm((DEPTH, 6 * D), 0.02)
    norm_mix_g = 1.0 + nrm((DEPTH, D), 0.02)
    norm_ffn_g = 1.0 + nrm((DEPTH, D), 0.02)
    final_g = 1.0 + nrm((D,), 0.02)
    gdn_w_in = nrm((nA, D, GDN_PROJ), D ** -0.5)
    gdn_conv_w = nrm((nA, GDN_CONV, 2 * GDN_HEADS * GDN_DK + GDN_HEADS * GDN_DV), GDN_CONV ** -0.5)
    gdn_a_log = jnp.log(jax.random.uniform(next(ks), (nA, 2, GDN_HEADS), jnp.float32, 1.0, 16.0))
    dt = jnp.exp(jax.random.uniform(next(ks), (nA, 2, GDN_HEADS), jnp.float32, math.log(1e-3), math.log(1e-1)))
    gdn_dt_bias = dt + jnp.log(-jnp.expm1(-dt))
    gdn_norm_g = 1.0 + nrm((nA, GDN_DV), 0.02)
    gdn_w_out = nrm((nA, GDN_HEADS * GDN_DV, D), (GDN_HEADS * GDN_DV) ** -0.5)
    mlstm_w_in = nrm((nB, D, MLSTM_PROJ), D ** -0.5)
    mlstm_b_i = nrm((nB, 2, MLSTM_HEADS), 0.1)
    mlstm_b_f = jnp.linspace(3.0, 6.0, MLSTM_HEADS, dtype=jnp.float32)[None, None, :] + nrm((nB, 2, MLSTM_HEADS), 0.1)
    mlstm_norm_g = 1.0 + nrm((nB, MLSTM_DV), 0.02)
    mlstm_w_out = nrm((nB, MLSTM_HEADS * MLSTM_DV, D), (MLSTM_HEADS * MLSTM_DV) ** -0.5)
    diff_w_in = nrm((nC, D, DIFF_PROJ), D ** -0.5)
    diff_lambda = nrm((nC, 4, DIFF_DH), 0.1)
    diff_norm_g = 1.0 + nrm((nC, 2 * DIFF_DH), 0.02)
    diff_w_out = nrm((nC, 2 * DIFF_HEADS * DIFF_DH, D), (2 * DIFF_HEADS * DIFF_DH) ** -0.5)
    swa_w_in = nrm((nD, D, SWA_PROJ), D ** -0.5)
    swa_sink = nrm((nD, SWA_QHEADS), 0.5)
    swa_w_out = nrm((nD, SWA_QHEADS * SWA_DH, D), (SWA_QHEADS * SWA_DH) ** -0.5)
    router_w = nrm((DEPTH, D, N_EXPERTS), D ** -0.5)
    router_b = nrm((DEPTH, N_EXPERTS), 0.01)
    moe_w_gu = nrm((DEPTH, N_EXPERTS, D, 2 * D_FF), D ** -0.5)
    moe_b_gu = nrm((DEPTH, N_EXPERTS, 2 * D_FF), 0.01)
    moe_w_down = nrm((DEPTH, N_EXPERTS, D_FF, D), D_FF ** -0.5)
    moe_b_down = nrm((DEPTH, N_EXPERTS, D), 0.01)
    return {'x': x, 'c': c, 'ctx': ctx, 'c_ctx': c_ctx, 'ada_w': ada_w, 'ada_b': ada_b,
            'norm_mix_g': norm_mix_g, 'norm_ffn_g': norm_ffn_g, 'final_g': final_g,
            'gdn_w_in': gdn_w_in, 'gdn_conv_w': gdn_conv_w, 'gdn_a_log': gdn_a_log, 'gdn_dt_bias': gdn_dt_bias,
            'gdn_norm_g': gdn_norm_g, 'gdn_w_out': gdn_w_out,
            'mlstm_w_in': mlstm_w_in, 'mlstm_b_i': mlstm_b_i, 'mlstm_b_f': mlstm_b_f,
            'mlstm_norm_g': mlstm_norm_g, 'mlstm_w_out': mlstm_w_out,
            'diff_w_in': diff_w_in, 'diff_lambda': diff_lambda, 'diff_norm_g': diff_norm_g, 'diff_w_out': diff_w_out,
            'swa_w_in': swa_w_in, 'swa_sink': swa_sink, 'swa_w_out': swa_w_out,
            'router_w': router_w, 'router_b': router_b, 'moe_w_gu': moe_w_gu, 'moe_b_gu': moe_b_gu,
            'moe_w_down': moe_w_down, 'moe_b_down': moe_b_down}

def reference(x, c, ctx, c_ctx, ada_w, ada_b, norm_mix_g, norm_ffn_g, final_g,
              gdn_w_in, gdn_conv_w, gdn_a_log, gdn_dt_bias, gdn_norm_g, gdn_w_out,
              mlstm_w_in, mlstm_b_i, mlstm_b_f, mlstm_norm_g, mlstm_w_out,
              diff_w_in, diff_lambda, diff_norm_g, diff_w_out,
              swa_w_in, swa_sink, swa_w_out,
              router_w, router_b, moe_w_gu, moe_b_gu, moe_w_down, moe_b_down):
    B, L, D = x.shape
    Lc = ctx.shape[1]
    rope = _axial_rope_tables(L, DIFF_DH)
    silu_c = jax.nn.silu(c)
    silu_cc = jax.nn.silu(c_ctx)
    xc = ctx
    for i in range(DEPTH):
        last = i == DEPTH - 1
        kind, j = i % N_MIXERS, i // N_MIXERS
        mx = jnp.split(silu_c @ ada_w[i] + ada_b[i], 6, axis=-1)
        sh1x, sc1x, g1x, sh2x, sc2x, g2x = [m[:, None, :] for m in mx]
        sh1c, sc1c, g1c, sh2c, sc2c, g2c = jnp.split(silu_cc @ ada_w[i] + ada_b[i], 6, axis=-1)
        hx = _modulate(_rmsnorm(x, norm_mix_g[i]), sh1x, sc1x)
        hc = _modulate(_rmsnorm(xc, norm_mix_g[i]), sh1c, sc1c)
        if kind == 0:
            yc, yx = _gdn_mixer(hc, hx, gdn_w_in[j], gdn_conv_w[j], gdn_a_log[j], gdn_dt_bias[j],
                                gdn_norm_g[j], gdn_w_out[j], not last)
        elif kind == 1:
            yc, yx = _mlstm_mixer(hc, hx, mlstm_w_in[j], mlstm_b_i[j], mlstm_b_f[j], mlstm_norm_g[j],
                                  mlstm_w_out[j], not last)
        elif kind == 2:
            lambda_init = 0.8 - 0.6 * math.exp(-0.3 * i)
            yc, yx = _diff_mixer(hc, hx, diff_w_in[j], diff_lambda[j], diff_norm_g[j], diff_w_out[j],
                                 rope, lambda_init, not last)
        else:
            yc, yx = _swa_mixer(hc, hx, swa_w_in[j], swa_sink[j], swa_w_out[j], rope, not last)
        x = x + g1x * yx
        fx = _modulate(_rmsnorm(x, norm_ffn_g[i]), sh2x, sc2x).reshape(B * L, D)
        if last:
            x = x + g2x * _moe(fx, router_w[i], router_b[i], moe_w_gu[i], moe_b_gu[i],
                               moe_w_down[i], moe_b_down[i]).reshape(B, L, D)
        else:
            xc = xc + g1c * yc
            fc = _modulate(_rmsnorm(xc, norm_ffn_g[i]), sh2c, sc2c).reshape(B * Lc, D)
            fo = _moe(jnp.concatenate([fx, fc], axis=0), router_w[i], router_b[i], moe_w_gu[i], moe_b_gu[i],
                      moe_w_down[i], moe_b_down[i])
            x = x + g2x * fo[:B * L].reshape(B, L, D)
            xc = xc + g2c * fo[B * L:].reshape(B, Lc, D)
    return _rmsnorm(x, final_g)


_drawn_inputs = setup_inputs


def setup_inputs(seed=0):
    import zlib

    import numpy as np

    out = dict(_drawn_inputs(seed))
    spreads = {}
    factors = {'c_ctx': 3.795,
     'norm_mix_g': 5.128,
     'norm_ffn_g': 15.033,
     'final_g': 27.716,
     'gdn_norm_g': 6.25,
     'router_b': 37.02,
     'moe_b_gu': 58.359,
     'moe_b_down': 200.0}
    for name, (base, spread) in spreads.items():
        noise = np.random.default_rng([zlib.crc32(name.encode()), seed]).standard_normal(out[name].shape)
        drawn = base * np.exp(spread * noise) if base else spread * noise
        out[name] = jnp.asarray(drawn.astype(out[name].dtype))
    for name, factor in factors.items():
        out[name] = (out[name] * factor).astype(out[name].dtype)
    return out
```

```python
from contextlib import ExitStack

import concourse.bass as bass
from concourse import mybir

F32 = mybir.dt.float32
BF16 = mybir.dt.bfloat16
U32 = mybir.dt.uint32
I32 = mybir.dt.int32
ALU = mybir.AluOpType
ACT = mybir.ActivationFunctionType
AX = mybir.AxisListType

P = 128
D = 1024
KT = D // P
SEQ = 512
CTX = 256
H = 8
NC = CTX // P
NL = SEQ // P
C = NC + NL
E = 32
FF = 1024
TOPK = 4
BLK = 64
NBLK = SEQ * TOPK // BLK + E
EPS = 1e-6
LEVELS = (1, 2, 4, 8, 16, 32, 64)
CONV = 5
ORDER = (list(range(C)), list(range(NC))[::-1] + list(range(NC, C))[::-1])


def tcol(c):
    return c * P if c < NC else CTX + 4 + (c - NC) * P


class Signal:

    def __init__(self, sem, tags, unit=1, before=0):
        self.sem, self.tags, self.unit, self.before = sem, list(tags), unit, before
        self.at = {t: i + 1 for i, t in enumerate(self.tags)}
        self.next = 0

    def value(self, h, tag):
        return (h * len(self.tags) + (self.at[tag] + self.before)) * self.unit

    def wait(self, eng, h, tag):
        eng.wait_ge(self.sem, self.value(h, tag))

    def done(self, ins, tag):
        assert self.tags[self.next % len(self.tags)] == tag, (tag, self.tags[self.next % len(self.tags)])
        self.next += 1
        return ins.then_inc(self.sem, self.unit)


class Banks:

    def __init__(self, banks, full, drained, tags, before=None):
        self.banks, self.full, self.drained = banks, full, drained
        self.tags, self.n = list(tags), len(banks)
        self.before = before or [0] * self.n
        assert len(self.tags) % self.n == 0
        self.at = {t: i for i, t in enumerate(self.tags)}

    def bank(self, tag):
        return self.banks[self.at[tag] % self.n]

    def count(self, h, tag):
        i = self.at[tag]
        return h * (len(self.tags) // self.n) + (self.before[i % self.n] + i // self.n)

    def open(self, pe, h, tag):
        v = self.count(h, tag)
        if not (isinstance(v, int) and v == 0):
            pe.wait_ge(self.drained[self.at[tag] % self.n], v)
        return self.bank(tag)

    def close(self, ins, tag):
        ins.then_inc(self.full[self.at[tag] % self.n], 1)

    def wait_full(self, eng, h, tag):
        eng.wait_ge(self.full[self.at[tag] % self.n], self.count(h, tag) + 1)
        return self.bank(tag)

    def release(self, ins, tag):
        ins.then_inc(self.drained[self.at[tag] % self.n], 1)

    def wait_drained(self, eng, h, tag):
        eng.wait_ge(self.drained[self.at[tag] % self.n], self.count(h, tag) + 1)


def trunk(nc, x, c, ctx_tokens, c_ctx, ada_w, ada_b, norm_mix_g, norm_ffn_g, final_g, w_in, conv_w, a_log,
          dt_bias, norm_g, w_out, router_w, router_b, w_gu, b_gu, w_down, b_down, out):
    with ExitStack() as stack:
        def sb(name, shape, dt=F32):
            return stack.enter_context(nc.sbuf_tensor(name, shape, dt))

        def sem(name):
            return stack.enter_context(nc.semaphore(name))

        def sems(name, n):
            return [sem(f"{name}{i}") for i in range(n)]

        SLOT = 4096
        NSLOT = 8
        ring = sb("ring", [P, NSLOT * SLOT])
        cursor = [0]

        def carve(n, at=None):
            if at is not None:
                cursor[0] = at
            a = ring[:, cursor[0]:cursor[0] + n]
            cursor[0] += n
            assert cursor[0] <= NSLOT * SLOT
            return a

        x_sb = sb("x_sb", [P, NL, D])
        ident = sb("ident", [P, P])
        ones = sb("ones", [P, P])
        tri = sb("tri", [P, 4, P])
        LE, GE, GT, LT = range(4)
        cols = sb("cols", [P, 82])
        ada = sb("ada", [P, 48, 2])
        ada_mod = sb("ada_mod", [P, KT, 2])
        stat = sb("stat", [P, 64])
        bias = sb("bias", [3 * E, 3 * FF], BF16)
        pick = sb("pick", [3 * E, E], BF16)
        pick_now = sb("pick_now", [3 * E, BLK], BF16)
        a_front = sb("a_front", [P, 6144 + 4096])
        hT = a_front[:, 0:6144].rearrange("p (k t) -> p k t", k=KT)
        oT = a_front[:, 6144:10240].rearrange("p (h t) -> p h t", h=H)
        lvl = sb("lvl", [P, len(LEVELS), 2, P])
        decays = sb("decays", [P, 72, H])
        convc = sb("convc", [P, 120])
        gates = sb("gates", [P, NL, TOPK])
        yrow_of = sb("yrow_of", [P, NL * TOPK], U32)
        tok_of = sb("tok_of", [BLK, NBLK + 2], U32)
        tok_now = sb("tok_now", [BLK, 1], U32)
        plan = sb("plan", [1, 3 * E + 1], I32)

        af = lambda a, n: a_front[:, a:a + n]
        diag = af(0, D).rearrange("p (k n) -> p k n", k=KT)
        tmp = af(0, D)
        g1b = af(1024, D)
        g2b = af(2048, D)
        xn2 = [af(3072, D), af(4096, D)]
        h2T = af(5120, D).rearrange("p (k n) -> p k n", k=KT)
        xg = a_front[0:BLK, 0:D]
        yrow = af(1024, 512)
        glu, sig, lin, act_rows = (af(3072 + 512 * i, 512) for i in range(4))
        act_T = af(5120, 512).rearrange("p (j h t) -> p j h t", j=4, h=2)
        xT = af(5632, 512).rearrange("p (f t) -> p f t", f=8)
        OE = af(6144, 512).rearrange("p (i k e) -> p i k e", i=NL, k=TOPK)
        M = af(6656, 128).rearrange("p (i e) -> p i e", i=NL)
        slot_of = af(6784, 128).rearrange("p (i e) -> p i e", i=NL)
        lg = af(6912, 128).rearrange("p (i e) -> p i e", i=NL)
        top = af(7040, 32).rearrange("p (i k) -> p i k", i=NL)
        topi = af(7072, 32).bitcast(U32).rearrange("p (i k) -> p i k", i=NL)
        topf = af(7104, 16).rearrange("p (i k) -> p i k", i=NL)
        ex = af(7120, 16).rearrange("p (i k) -> p i k", i=NL)
        exs = af(7136, 8)
        nbf = af(7144, E)
        bsf = af(7176, E)
        cnt = af(7208, E)
        dest = af(7240, 16)
        desti = af(7256, 16).bitcast(I32)
        blki = af(7272, 16).bitcast(I32)
        sloti = af(7288, 16).bitcast(I32)
        blkf = af(7304, 16)
        slotf = af(7320, 16)
        ss2 = stat[:, 32:64]
        prod = af(7424, 512).rearrange("p (i k e) -> p i k e", i=NL, k=TOPK)
        OS = af(8192, 1024).rearrange("p (j s) -> p j s", s=BLK)
        OB = af(9216, 1024).rearrange("p (j s) -> p j s", s=BLK)
        fg = af(8192, D)
        zero_rows = a_front[:, 6144:6144 + D]
        first_rows = [af(8192 + 512 * i, 512) for i in range(4)]
        gate_rows = af(8192, CTX + SEQ)
        tail = lvl[:].rearrange("p l d i -> p (l d i)")
        rw = tail[:, 0:256].rearrange("p (k e) -> p k e", k=KT)
        rb = tail[:, 256:288]
        iota64 = tail[:, 288:352]
        tokid = tail[:, 352:356]
        sqj = tail[:, 512:1536]
        wout = ring[:, 6 * SLOT:8 * SLOT].rearrange("p (h n) -> p h n", h=H)
        slots = [ring[:, i * SLOT:(i + 1) * SLOT].rearrange("p (k n) -> p k n", k=8) for i in range(NSLOT)]
        got = [ring[:, j * D:(j + 1) * D] for j in range(NL * TOPK)]
        osum = [ring[:, (16 + i) * D:(17 + i) * D] for i in range(NL)]
        ofin = [ring[:, (20 + i) * D:(21 + i) * D] for i in range(NL)]

        adaw = carve(SLOT, 6 * SLOT).rearrange("p (k n) -> p k n", k=KT)
        win = carve(SLOT, 7 * SLOT).rearrange("p (q k n) -> p q k n", q=4, k=KT)
        first_ada = [carve(SLOT, i * SLOT).rearrange("p (k n) -> p k n", k=KT) for i in range(4)]
        ctx_sb = carve(NC * D, 4 * SLOT).rearrange("p (c d) -> p c d", c=NC)
        xn = [carve(D), carve(D)]
        junk = carve(D, 5 * SLOT)
        rows = carve(2 * P)
        wgate = carve(KT * 32).rearrange("p (k n) -> p k n", k=KT)
        gate = carve(C * 32).rearrange("p (c n) -> p c n", c=C)
        ga = [carve(C * 16).rearrange("p (c n) -> p c n", c=C) for _ in range(4)]
        rates = carve(48)
        GATE_END = cursor[0]
        assert GATE_END <= 6 * SLOT

        pre_q = carve(SEQ + 4, 0)
        pre_k = carve(CTX + SEQ + 8)
        pre_v = carve(CTX + SEQ + 8)
        qT = carve(SEQ)
        kT = carve(CTX + SEQ + 4)
        vT = carve(CTX + SEQ + 4)
        sq_q = carve(SEQ)
        sq_k = carve(CTX + SEQ + 4)
        conv_q, conv_k = sq_q, sq_k
        Kn = carve(C * P).rearrange("p (c n) -> p c n", c=C)
        bias_rows = ring[0:3 * E, 2 * SLOT:2 * SLOT + 3 * FF]
        bias_rest = ring[0:3 * E, 3 * SLOT:3 * SLOT + 3 * FF]
        Vn = carve(C * P).rearrange("p (c n) -> p c n", c=C)
        zs = carve(NL * P).rearrange("p (c n) -> p c n", c=NL)
        GU = [carve(512).rearrange("p (u i) -> p u i", u=4) for _ in range(2)]
        gam = [carve(512).rearrange("p (u i) -> p u i", u=4) for _ in range(3)]
        gamI = [carve(512).rearrange("p (u i) -> p u i", u=4) for _ in range(2)]
        AT = [carve(512).rearrange("p (u i) -> p u i", u=4) for _ in range(3)]
        PT = [carve(512).rearrange("p (u i) -> p u i", u=4) for _ in range(2)]
        X = [carve(512).rearrange("p (u i) -> p u i", u=4) for _ in range(3)]
        T = [carve(512).rearrange("p (u i) -> p u i", u=4) for _ in range(3)]
        Lm = [[carve(512).rearrange("p (u i) -> p u i", u=4) for _ in range(2)] for _ in range(3)]
        Pb = [carve(512).rearrange("p (u i) -> p u i", u=4) for _ in range(3)]
        oacc = carve(NL * P).rearrange("p (c n) -> p c n", c=NL)
        S = carve(256).rearrange("p (d n) -> p d n", d=2)
        R = carve(256).rearrange("p (d n) -> p d n", d=2)
        vP = carve(256).rearrange("p (d n) -> p d n", d=2)
        vS = carve(256).rearrange("p (d n) -> p d n", d=2)
        on = carve(NL * P).rearrange("p (c n) -> p c n", c=NL)
        hc = carve(72).rearrange("p (q d c) -> p q d c", q=6, d=2)
        cw = carve(15)
        gc = carve(12).rearrange("p (d c) -> p d c", d=2)
        ssc = carve(10)
        nrm = carve(10)
        r2 = carve(C)
        c1 = carve(12).rearrange("p (d c) -> p d c", d=2)
        c3 = carve(12).rearrange("p (d c) -> p d c", d=2)
        ofac = carve(24)
        ada_rows = carve(512)
        sc = ring[:, 6 * SLOT - 256:6 * SLOT].rearrange("p (k m) -> p k m", k=KT)
        group_sum = ring[:, 6 * SLOT - 288:6 * SLOT - 256]
        assert max(cursor[0], GATE_END) <= 6 * SLOT - 288, cursor[0]

        bank = [stack.enter_context(nc.psum_tensor(f"bank{i}", [P, 512], F32)) for i in range(8)]
        scan_tags = []
        for t in range(C):
            scan_tags += ([("ks", t)] if t else []) + [("y", t)] + ([("su", t)] if t < C - 1 else []) \
                + ([("o", t)] if t >= NC else [])
        items = [(l, g) for l in range(1, len(LEVELS)) for g in range(3)]
        pa = Banks([bank[0], bank[1]], sems("pa_full", 2), sems("pa_drained", 2),
                   ["k", "kc", "v", "vc", "q", "z"])
        inverse_tags = [("P", *items[0]), ("P", *items[1])]
        for n, (l, g) in enumerate(items):
            inverse_tags += ([("T", *items[n - 1])] if n and items[n - 1][0] < len(LEVELS) - 1 else []) \
                + ([("P", *items[n + 2])] if n + 2 < len(items) else [])
        pb = Banks([bank[2], bank[3], bank[7]], sems("pb_full", 3), sems("pb_drained", 3),
                   ["kt0", "kt1", "vt"] + [("dt", g) for g in range(3)] + inverse_tags
                   + ["adar", "ada0", "ada1", "ada2", "ada3", "ot"], before=[3, 3, 1])
        pc_tags = ["ss"] + [("kq", g) for g in range(3)] + [("lt", g) for g in range(3)] + [("X", *i) for i in items]
        pc = Banks([bank[4 + i] for i in range(3)], sems("pc_full", 3), sems("pc_drained", 3),
                   pc_tags + scan_tags, before=[2, 2, 2])

        s_rows = sem("rows_loaded")
        s_small = sem("small_loaded")
        s_x = sem("x_loaded")
        s_adaw = sems("first_ada_loaded", 4)
        s_wgate = sem("gate_weights_loaded")
        s_pool = sem("constants_made")
        s_fps = sem("front_psum_full")
        s_fv = sem("front_vector_done")
        s_fs = sem("front_scalar_done")
        s_pads = sem("pads_zeroed")
        s_zc = sem("columns_zeroed")
        s_sum = sem("group_sum_made")
        s_rfull = sem("first_rows_full")
        s_rcopy = sem("first_rows_copied")
        s_gfull = sem("gate_rows_full")
        s_gcopy = sem("gate_rows_copied")
        s_brows = sem("bias_rows_loaded")
        s_bias = sem("bias_split")
        s_mid = sem("middle_bias_copied")

        win_loaded = sems("win_loaded", 4)
        ada_loaded = sem("ada_loaded")
        convd = Signal(sem("conv_taps"), [(s, k) for s in (1, 2, 0) for k in range(CONV)])
        silu = Signal(sem("silu_done"), ["k", "v", "q", "sqk", "sqq", "nrm"])
        colsig = Signal(sem("head_columns"), ["hc"])
        tapsig = Signal(sem("head_taps"), ["cw", "gc"])
        small = Signal(sem("norm_columns"), ["r2", "rq", "c1", "c3"])
        GUd = Signal(sem("decay_rows"), [0, 1])
        GUlast = Signal(sem("last_decay_rows"), [2])
        lm0 = Signal(sem("first_level_masked"), [0, 1, 2])
        gammask = Signal(sem("decay_masked"), [1, 2])
        lmsig = Signal(sem("level_masked"), [(l, g) for l in range(1, len(LEVELS)) for g in range(3)])
        x0 = Signal(sem("first_inverse"), [0, 1, 2])
        atd = Signal(sem("systems"), [1, 2])
        scan = Signal(sem("scan_steps"), [(x, t) for t in range(NC, C) for x in ("R", "vS")])
        post = Signal(sem("head_normalised"), ["a", "a2", "m", "var", "rstd", "fac", "on"])
        postA = Signal(sem("head_squares"), ["ss", "sqrt"])
        oTd = Signal(sem("head_outputs"), ["oT"])

        xs = nc.dram_tensor("xs", (SEQ, D), F32, kind="Internal").ap()
        ys = nc.dram_tensor("ys", (NBLK * BLK, D), F32, kind="Internal").ap()

        pe_tags = ["g1", "g2"]
        pe_tags += [("wo", 0), ("wo", 1), ("wo", 2), ("tr", 0), ("wo", 3), ("tr", 1), ("lo", 0), ("tr", 2), ("lo", 1),
                    ("tr", 3), ("lo", 2), ("lo", 3)]
        PT_ = Signal(sem("route_tensor"), pe_tags + ["pos", "ids"])
        v_tags = ["ada2", "A2", "dg1", "g1b", "dg2", "g2b"]
        for a in range(NL + 1):
            if a < NL:
                v_tags += [("m", a), ("x", a)]
            if a:
                v_tags += [("var", a - 1), ("rs", a - 1), ("xn", a - 1)]
        for i in range(NL):
            v_tags += [("lg", i), ("top", i), ("topi", i)]
        v_tags += ["topf", "sub", "OE", "M", "sum", "rec", "gates"] + [("nb", j) for j in range(8)] \
            + ["bsi", "bs", "plan", "dst", "prod", "dest", "yrow", "desti", "blki", "sloti", "blkf", "slotf", "OS", "OB",
               "OBt", "tok_of"]
        VT = Signal(sem("route_vector"), v_tags)
        AT_ = Signal(sem("route_scalar"), [x for i in range(NL) for x in (("ss", i), ("sq", i))]
                     + [("h2T", i) for i in range(NL)] + ["exp"])
        s_wout = sem("wout_loaded")
        s_rw = sem("router_loaded")
        s_iota = sem("iotas_made")
        s_store = sems("tokens_stored", NL)
        s_fill = sem("spare_blocks_filled")
        s_fg = sem("final_norm_loaded")

        slot_loaded = sems("slot_loaded", NSLOT)
        PEs = Signal(sem("expert_tensor"), ["g", "l0", "l1", "xt", "at0", "at1", "d"], before=1)
        DVs = Signal(sem("expert_vector"), ["glu", "m", "c0", "act0", "c1", "act1", "xa", "xb"], before=2)
        s_pick = sem("bias_picked")
        ACs = Signal(sem("expert_scalar"), ["sig", "at0", "at1", "y"])
        s_tokcol = sem("block_tokens_ready")
        s_gather = sem("rows_gathered")
        s_ystore = sem("rows_stored")

        s_back = sems("rows_back", NL * TOPK)
        e_tags = []
        for i in range(NL):
            e_tags += [("c", i, k) for k in range(TOPK)] + [("g", i), ("x", i)]
            if i:
                e_tags += [("var", i - 1), ("rs", i - 1), ("out", i - 1)]
        e_tags += [("var", NL - 1), ("rs", NL - 1), ("out", NL - 1)]
        VE = Signal(sem("end_vector"), e_tags)
        AE = Signal(sem("end_scalar"), [x for i in range(NL) for x in (("ss", i), ("sq", i))])
        s_out = sem("output_stored")

        FV_MOD, FV_U, FV_GB, FV_G = 6, 11, 12, 15
        adaw_view = ada_w[0].rearrange("(k p) n -> p k n", p=P)
        win_view = w_in[0].rearrange("(k p) n -> p k n", p=P)

        block = stack.enter_context(nc.Block())

        @block.sync
        def _(sp):
            sp.dma_start(rows[0:8, 0:P], c[0].rearrange("(r p) -> r p", p=P)).then_inc(s_rows, 16)
            sp.dma_start(rows[8:16, 0:P], c_ctx.rearrange("(r p) -> r p", p=P)).then_inc(s_rows, 16)
            sp.dma_start(rows[16:24, 0:P], norm_mix_g[0].rearrange("(r p) -> r p", p=P)).then_inc(s_rows, 16)
            sp.dma_start(rows[24:32, 0:P], norm_ffn_g[0].rearrange("(r p) -> r p", p=P)).then_inc(s_rows, 16)
            sp.dma_start(rows[32:33, 0:P], norm_g).then_inc(s_rows, 16)
            sp.dma_start(rows[33:81, 0:P], ada_b[0].rearrange("(r p) -> r p", p=P)).then_inc(s_rows, 16)
            for i in range(4):
                sp.dma_start(first_ada[i], adaw_view[:, :, i * 512:(i + 1) * 512]).then_inc(s_adaw[i], 16)
            sp.dma_start(wgate, win_view[:, :, 4096:4128]).then_inc(s_wgate, 16)

            def load_win(h, q):
                sp.dma_start(win[:, q], win_view[:, :, bass.ds(q * D + h * P, P)]).then_inc(win_loaded[q], 16)

            for q in (1, 2, 0, 3):
                load_win(0, q)
            sp.wait_ge(s_fps, 3)
            for r in range(3):
                rr = slice(r * E, (r + 1) * E)
                sp.dma_start(bias_rows[rr, 0:2 * FF], b_gu[0]).then_inc(s_brows, 16)
                sp.dma_start(bias_rows[rr, 2 * FF:3 * FF], b_down[0]).then_inc(s_brows, 16)
            sp.dma_start(adaw, adaw_view[:, :, 2048:2560]).then_inc(ada_loaded, 16)
            with sp.Fori(0, H - 1) as h:
                for q, last_use in enumerate(("q", "kc", "vc", "z")):
                    pa.wait_full(sp, h, last_use)
                    load_win(h + 1, q)
                pb.wait_full(sp, h, "adar")
                sp.dma_start(adaw, adaw_view[:, :, bass.ds(2560 + h * 512, 512)]).then_inc(ada_loaded, 16)
            pb.wait_full(sp, H - 1, "adar")
            pa.wait_full(sp, H - 1, "z")
            sp.dma_start(wout, w_out[0].rearrange("(h p) n -> p h n", p=P)).then_inc(s_wout, 16)
            pb.wait_full(sp, H - 1, "ot")
            sp.dma_start(rw, router_w[0].rearrange("(k p) e -> p k e", p=P)).then_inc(s_rw, 16)
            sp.dma_start(rb, router_b.to_broadcast([P, E])).then_inc(s_rw, 16)

            gu_view = w_gu[0].rearrange("e (k p) n -> e p k n", p=P)
            dn_view = w_down[0].rearrange("e (k p) n -> e p k n", p=P)

            def load_chunk(slot, e, q):
                view, col = (gu_view, q * 512) if q < 4 else (dn_view, (q - 4) * 512)
                src = view[e] if isinstance(e, int) else view[bass.ds(e, 1)].rearrange("a p k n -> (a p) k n")
                sp.dma_start(slots[slot], src[:, :, col:col + 512]).then_inc(slot_loaded[slot], 16)

            for q in range(6):
                load_chunk(q, 0, q)
            for i in range(NL):
                VT.wait(sp, 0, ("xn", i))
                sp.dma_start(xs[i * P:(i + 1) * P, :], xn2[i % 2]).then_inc(s_store[i], 16)
            PT_.wait(sp, 0, ("wo", NL - 1))
            for q in range(2):
                load_chunk(6 + q, 1, q)
            PT_.wait(sp, 0, "ids")
            sp.dma_start(fg, final_g.rearrange("(a n) -> a n", a=1).to_broadcast([P, D])).then_inc(s_fg, 16)
            VT.wait(sp, 0, "plan")

            def four(i, count):
                for m in range(count):
                    if m % 6 == 0:
                        e = 4 * i + m // 6
                        last = sp.value_load(plan[0:1, bass.ds(e + 2 * E, 1)], min_val=0, max_val=NBLK - 1)
                    PEs.wait(sp, last, ("g", "l1", "d")[m % 6 // 2])
                    load_chunk(m % NSLOT, 4 * i + (m + 8) // 6, (m + 8) % 6)

            with sp.Fori(0, E // 4 - 1) as i:
                four(i, 24)
            four(E // 4 - 1, 16)
            for i in range(NL):
                VE.wait(sp, 0, ("out", i))
                sp.dma_start(out[0, i * P:(i + 1) * P, :], ofin[i]).then_inc(s_out, 16)
            sp.wait_ge(s_out, 16 * NL)

        @block.gpsimd
        def _(pool):
            n = [0]

            def mark(ins):
                n[0] += 1
                return ins.then_inc(s_pool, 1)

            pool.memset(sc, 0.0).then_inc(s_zc, 1)
            mark(pool.memset(ones[:], 1.0))
            mark(pool.memset(ident[:], 0.0))
            mark(pool.memset(tri[:], 1.0))
            mark(pool.memset(lvl[:], 0.0))
            mark(pool.memset(zero_rows, 0.0))
            pool.wait_ge(s_pool, n[0])
            mark(pool.affine_select(out=ident[:], in_=ident[:], compare_op=ALU.not_equal, fill=1.0, base=0,
                                    pattern=[[-1, P]], channel_multiplier=1))
            for m, (a, b, base) in enumerate(((-1, 1, 0), (1, -1, 0), (1, -1, -1), (-1, 1, -1))):
                mark(pool.affine_select(out=tri[:, m, :], in_=tri[:, m, :], compare_op=ALU.is_ge, fill=0.0,
                                        base=base, pattern=[[b, P]], channel_multiplier=a))
            for l, s in enumerate(LEVELS):
                for d in range(2):
                    v = lvl[:, l, d, :].rearrange("p (a h r) -> p a h r", h=2, r=s)[:, :, 1 - d, :]
                    mark(pool.memset(v, 1.0))
            pool.wait_ge(s_pool, n[0])
            for l, s in enumerate(LEVELS):
                for d in range(2):
                    v = lvl[:, l, d, :].rearrange("p (a h r) -> p a h r", h=2, r=s)[:, :, 1 - d, :]
                    blocks = P // (2 * s)
                    mark(pool.affine_select(out=v, in_=v, compare_op=ALU.is_ge, fill=0.0, base=-d * s,
                                            pattern=[[-2 * s, blocks], [0, s]], channel_multiplier=1))
                    pool.wait_ge(s_pool, n[0])
                    mark(pool.affine_select(out=v, in_=v, compare_op=ALU.is_ge, fill=0.0, base=d * s + s - 1,
                                            pattern=[[2 * s, blocks], [0, s]], channel_multiplier=-1))

            mark(pool.memset(pick[:], 0.0))
            pool.wait_ge(s_pool, n[0])
            for r in range(3):
                rr = slice(r * E, (r + 1) * E)
                mark(pool.affine_select(out=pick[rr, :], in_=pick[rr, :], compare_op=ALU.not_equal, fill=1.0, base=0,
                                        pattern=[[-1, E]], channel_multiplier=1))
                pool.wait_ge(s_pool, n[0])
            pool.dma_start(ys[E * BLK:, :].rearrange("(p r) n -> p r n", p=P),
                           zero_rows.unsqueeze(1).to_broadcast([P, E * BLK // P, D])).then_inc(s_fill, 16)
            pool.wait_ge(s_brows, 96)
            pool.tensor_copy(bias[:], bias_rows).then_inc(s_bias, 1)
            pool.wait_ge(s_bias, 1)
            pool.tensor_tensor(bias_rest, bias_rows, bias[:], ALU.subtract).then_inc(s_bias, 1)
            pool.wait_ge(s_bias, 2)
            low = slice(2 * E, 3 * E)
            pool.tensor_copy(bias[low, :], bias_rest[low, :]).then_inc(s_bias, 1)
            pool.wait_ge(s_bias, 3)
            pool.tensor_tensor(bias_rest[low, :], bias_rest[low, :], bias[low, :], ALU.subtract).then_inc(s_bias, 1)
            pool.wait_ge(s_bias, 4)
            pool.tensor_copy(bias[low, :], bias_rest[low, :]).then_inc(s_bias, 1)
            pool.wait_ge(s_bias, 5)
            pool.wait_ge(s_mid, 1)

            def decay_rows(h, g):
                for d in range(2):
                    m = GE if d else LE
                    ins = pool.tensor_tensor(GU[g % 2][:, d::2, :], tri[:, m:m + 1, :].to_broadcast([P, 2, P]),
                                             gc[:, d, 2 * g:2 * g + 2].unsqueeze(2).to_broadcast([P, 2, P]), ALU.mult)
                (GUlast if g == 2 else GUd).done(ins, g)

            def first_rows_of(h):
                tapsig.wait(pool, h, "gc")
                for g in range(2):
                    decay_rows(h, g)

            def head(h, more):
                pb.wait_full(pool, h, ("dt", 0))
                decay_rows(h, 2)
                for g in (1, 2):
                    pb.wait_drained(pool, h, ("dt", g))
                    for d in range(2):
                        ins = pool.tensor_tensor(
                            gamI[g - 1][:, d::2, :], gam[g][:, d::2, :],
                            tri[:, (GE if d else LE):(GE if d else LE) + 1, :].to_broadcast([P, 2, P]), ALU.mult)
                    gammask.done(ins, g)
                for l in range(1, len(LEVELS)):
                    for g in range(3):
                        if l == 1:
                            lm0.wait(pool, h, g)
                        if l == 2:
                            pc.wait_full(pool, h, ("lt", g))
                            x0.wait(pool, h, g)
                        if l >= 3:
                            pb.wait_full(pool, h, ("P", l - 2, g))
                        lmsig.done(pool.tensor_tensor(
                            Lm[g][l % 2].rearrange("p (c d) i -> p c d i", d=2),
                            AT[g].rearrange("p (c d) i -> p c d i", d=2),
                            lvl[:, l:l + 1, :, :].to_broadcast([P, 2, 2, P]), ALU.mult), (l, g))
                        if l == 1:
                            x0.done(pool.tensor_tensor(X[g], ident[:].unsqueeze(1).to_broadcast([P, 4, P]),
                                                       Lm[g][0], ALU.subtract), g)
                if more:
                    pb.wait_full(pool, h, ("dt", 2))
                    first_rows_of(h + 1)

            pool.wait_ge(s_pool, n[0])
            first_rows_of(0)
            with pool.Fori(0, H - 1) as h:
                head(h, True)
            head(H - 1, False)

            pb.wait_full(pool, H - 1, ("P", 6, 2))
            pool.iota(iota64, pattern=[[1, BLK]], base=0, channel_multiplier=0,
                      allow_small_or_imprecise_dtypes=True).then_inc(s_iota, 1)
            pool.iota(tokid, pattern=[[P, NL]], base=0, channel_multiplier=1,
                      allow_small_or_imprecise_dtypes=True).then_inc(s_iota, 1)
            pool.memset(tok_of[:], 0).then_inc(s_iota, 1)

            for i in range(NL):
                pool.wait_ge(s_store[i], 16)
            VT.wait(pool, 0, "tok_of")
            n_blk = pool.value_load(plan[0:1, 3 * E:3 * E + 1], min_val=E, max_val=NBLK)

            def held(cell):
                pool.tensor_tensor(tail[0:1, cell:cell + 1], ones[0:1, 0:1], ones[0:1, 0:1], ALU.mult)

            def gather(b):
                pool.tensor_copy(tok_now[:], tok_of[:, bass.ds(b, 1)]).then_inc(s_tokcol, 1)
                pool.wait_ge(s_tokcol, b + 1)
                held(400)
                pool.indirect_dma_start(xg, None, xs, bass.IndirectOffsetOnAxis(ap=tok_now[:], axis=0)
                                        ).then_inc(s_gather, 16)

            gather(0)
            pool.wait_ge(PEs.sem, 1)
            gather(1)
            with pool.Fori(1, n_blk) as b:
                PEs.wait(pool, b - 1, "xt")
                gather(b + 1)

            pool.wait_ge(s_ystore, 32 * n_blk + 1)
            held(401)
            for j in range(NL * TOPK):
                pool.indirect_dma_start(got[j], None, ys, bass.IndirectOffsetOnAxis(ap=yrow_of[:, j:j + 1], axis=0)
                                        ).then_inc(s_back[j], 16)

        @block.scalar
        def _(act):
            act.dma_start(x_sb[:], x[0].rearrange("(c p) d -> p c d", p=P)).then_inc(s_x, 16)
            act.dma_start(ctx_sb, ctx_tokens[0].rearrange("(c p) d -> p c d", p=P)).then_inc(s_x, 16)
            act.dma_start(rows[0:120, P:2 * P], conv_w[0].rearrange("k (b p) -> (k b) p", p=P)).then_inc(s_small, 16)
            act.dma_start(rates[:, 0:16], a_log.rearrange("a d h -> a (d h)").to_broadcast([P, 16])).then_inc(s_small, 16)
            act.dma_start(rates[:, 16:32], dt_bias.rearrange("a d h -> a (d h)").to_broadcast([P, 16])).then_inc(s_small, 16)
            n = [0]

            def mark(ins):
                n[0] += 1
                return ins.then_inc(s_fs, 1)

            def chain(ins):
                mark(ins)
                act.wait_ge(s_fs, n[0])

            act.wait_ge(s_x, 32)
            for i in range(C):
                src = ctx_sb[:, i] if i < NC else x_sb[:, i - NC]
                chain(nc.scalar.activation(junk, src, ACT.Square, accum_out=stat[:, i:i + 1]))
            act.wait_ge(s_fv, 1)
            mark(nc.scalar.activation(stat[:, 8:14], stat[:, 8:14], ACT.Sqrt))
            act.wait_ge(s_fps, 1)
            mark(nc.scalar.activation(cols[:, 0:81], bank[0][:, 0:81], ACT.Copy))
            act.wait_ge(s_fs, n[0])
            act.wait_ge(s_zc, 1)
            mark(nc.scalar.activation(sc[:, :, 0:2], cols[:, 0:16].rearrange("p (s k) -> p k s", s=2), ACT.Silu))
            act.wait_ge(s_fps, 2)
            mark(nc.scalar.activation(convc[:], bank[1][:, 0:120], ACT.Copy))
            for i in range(4):
                act.wait_ge(s_rfull, i + 1)
                nc.scalar.activation(first_rows[i], bank[4 + i][:], ACT.Copy).then_inc(s_rcopy, 1)
            for i in range(C):
                act.wait_ge(s_fv, FV_MOD)
                act.wait_ge(pb.full[i % 2], i // 2 + 1)
                s = 1 if i < NC else 0
                for k in range(4):
                    ins = nc.scalar.activation(hT[:, k, i * P:(i + 1) * P], pb.banks[i % 2][:, k * P:(k + 1) * P],
                                               ACT.Identity, scale=ada_mod[:, k, s:s + 1], bias=ada[:, k, s:s + 1])
                ins.then_inc(pb.drained[i % 2], 1)
            act.wait_ge(s_small, 48)
            mark(nc.scalar.activation(rates[:, 32:48], rates[:, 0:16], ACT.Exp))
            act.wait_ge(s_fv, FV_U)
            chain(nc.scalar.activation(ga[1], ga[0], ACT.Abs))
            chain(nc.scalar.activation(ga[1], ga[1], ACT.Exp, scale=-1.0))
            mark(nc.scalar.activation(ga[1], ga[1], ACT.Ln, bias=1.0))
            act.wait_ge(s_fps, 5)
            for i in range(3):
                mark(nc.scalar.activation(decays[:, 24 + 12 * i:36 + 12 * i, :],
                                          bank[1][:, 96 * i:96 * i + 96].rearrange("p (q h) -> p q h", h=H),
                                          ACT.Exp))
            act.wait_ge(s_fv, FV_GB)
            mark(nc.scalar.activation(decays[:, 12:24, :].rearrange("p (d c) h -> p d c h", d=2),
                                      ga[3].rearrange("p c (d h) -> p d c h", d=2), ACT.Sigmoid))
            def modulation_columns(h):
                for n in range(4):
                    b = pb.wait_full(act, h, f"ada{n}")
                    pb.release(nc.scalar.activation(ada[:, bass.ds(16 + n + h * 4, 1), :],
                                                    b[:, 0:2].unsqueeze(1), ACT.Copy), f"ada{n}")

            def evacuate(h, first=False):
                for tag, dst, col, n_tok in (("k", pre_k, CTX + 6, SEQ), ("kc", pre_k, 2, CTX), ("v", pre_v, CTX + 6, SEQ),
                                             ("vc", pre_v, 2, CTX), ("q", pre_q, 2, SEQ)):
                    b = pa.wait_full(act, h, tag)
                    pa.release(nc.scalar.activation(dst[:, col:col + n_tok], b[:, 0:n_tok], ACT.Copy), tag)
                    if tag == "kc" and not first:
                        modulation_columns(h - 1)

            def head(h, more):
                for tag, s, src, a in (("k", 1, conv_k, kT), ("v", 2, vT, vT), ("q", 0, conv_q, qT)):
                    convd.wait(act, h, (s, CONV - 1))
                    silu.done(nc.scalar.activation(a, src, ACT.Silu), tag)
                silu.wait(act, h, "q")
                silu.done(nc.scalar.activation(sq_k, kT, ACT.Square), "sqk")
                silu.done(nc.scalar.activation(sq_q, qT, ACT.Square), "sqq")
                b = pb.wait_full(act, h, "kt0")
                pb.release(nc.scalar.activation(Kn[:, 0:4].rearrange("p c n -> p (c n)"), b[:], ACT.Copy), "kt0")
                pc.wait_drained(act, h, "ss")
                silu.done(nc.scalar.activation(nrm, ssc, ACT.Sqrt), "nrm")
                silu.wait(act, h, "nrm")
                b = pb.wait_full(act, h, "kt1")
                nc.scalar.activation(Kn[:, 4:6].rearrange("p c n -> p (c n)"), b[:, 0:256], ACT.Copy)
                nc.scalar.activation(Vn[:, 0], b[:, 256:384], ACT.Copy, scale=nrm[:, 0:1])
                pb.release(nc.scalar.activation(Vn[:, 1], b[:, 384:512], ACT.Copy, scale=nrm[:, 1:2]), "kt1")
                b = pb.wait_full(act, h, "vt")
                for i in range(4):
                    ins = nc.scalar.activation(Vn[:, 2 + i], b[:, i * P:(i + 1) * P], ACT.Copy, scale=nrm[:, 2 + i:3 + i])
                pb.release(ins, "vt")
                for g in range(3):
                    b = pb.wait_full(act, h, ("dt", g))
                    pb.release(nc.scalar.activation(gam[g].rearrange("p u i -> p (u i)"), b[:], ACT.Exp), ("dt", g))
                b = pa.wait_full(act, h, "z")
                pa.release(nc.scalar.activation(zs.rearrange("p c n -> p (c n)"), b[:], ACT.Silu), "z")
                for tag in inverse_tags:
                    b = pb.wait_full(act, h, tag)
                    dst = (Pb if tag[0] == "P" else T)[tag[2]]
                    pb.release(nc.scalar.activation(dst.rearrange("p u i -> p (u i)"), b[:], ACT.Copy), tag)
                b = pb.wait_full(act, h, "adar")
                pb.release(nc.scalar.activation(ada_rows, b[:], ACT.Copy), "adar")
                if more:
                    evacuate(h + 1)
                else:
                    modulation_columns(h)
                pc.wait_drained(act, h, ("o", C - 1))
                for i in range(NL):
                    ins = nc.scalar.activation(gam[0][:, i, :], oacc[:, i], ACT.Square, accum_out=ofac[:, i:i + 1])
                postA.done(ins, "ss")
                post.wait(act, h, "var")
                postA.done(nc.scalar.activation(ofac[:, 12:16], ofac[:, 8:12], ACT.Sqrt), "sqrt")
                b = pb.wait_full(act, h, "ot")
                pb.release(nc.scalar.activation(oT[:, bass.ds(h, 1), :].rearrange("p a t -> p (a t)"), b[:], ACT.Copy,
                                                scale=cols[:, 32:33]), "ot")

            act.wait_ge(s_bias, 2)
            nc.scalar.activation(bias[E:2 * E, :], bias_rest[E:2 * E, :], ACT.Copy).then_inc(s_mid, 1)
            evacuate(0, True)
            act.wait_ge(s_fill, 16)
            act.wait_ge(s_mid, 1)
            act.wait_ge(s_bias, 5)
            with act.Fori(0, H - 1) as h:
                head(h, True)
            head(H - 1, False)

            def h2t(i):
                PT_.wait(act, 0, ("tr", i))
                if i:
                    PT_.wait(act, 0, ("lo", i - 1))
                for k in range(KT):
                    ins = nc.scalar.activation(h2T[:, k, :], bank[(2 * i + k // 4) % 4][:, (k % 4) * P:(k % 4 + 1) * P],
                                               ACT.Identity, scale=ada_mod[:, k, 0:1], bias=ada[:, 24 + k, 0:1])
                AT_.done(ins, ("h2T", i))

            for i in range(NL):
                VT.wait(act, 0, ("x", i))
                if i:
                    AT_.wait(act, 0, ("ss", i - 1))
                AT_.done(nc.scalar.activation(sqj, x_sb[:, i], ACT.Square, accum_out=ss2[:, i:i + 1]), ("ss", i))
                VT.wait(act, 0, ("var", i))
                AT_.done(nc.scalar.activation(ss2[:, 8 + i:9 + i], ss2[:, 4 + i:5 + i], ACT.Sqrt), ("sq", i))
            for i in range(NL):
                h2t(i)
            VT.wait(act, 0, "sub")
            AT_.done(nc.scalar.activation(ex, ex, ACT.Exp), "exp")
            nc.scalar.activation(sqj[:, 0:1], ones[:, 0:1], ACT.Copy).then_inc(s_ystore, 1)

            VT.wait(act, 0, "plan")
            n_blk = act.value_load(plan[0:1, 3 * E:3 * E + 1], min_val=E, max_val=NBLK)

            with act.Fori(0, n_blk) as b:
                DVs.wait(act, b, "glu")
                ACs.done(nc.scalar.activation(sig, glu, ACT.Sigmoid, scale=1.702), "sig")
                for j in range(2):
                    PEs.wait(act, b, f"at{j}")
                    ACs.done(nc.scalar.activation(act_T[:, 2 * j:2 * j + 2].rearrange("p j h t -> p (j h t)"),
                                                  bank[4 + j][:, 0:256], ACT.Copy), f"at{j}")
                PEs.wait(act, b, "d")
                act.wait_ge(s_ystore, 32 * b + 1)
                ACs.done(nc.scalar.activation(yrow, bank[2][:], ACT.Copy), "y")
                ACs.wait(act, b, "y")
                for j in range(2):
                    act.dma_start(ys[bass.ds(b * BLK, BLK), j * 512:(j + 1) * 512],
                                  yrow[j * BLK:(j + 1) * BLK, :]).then_inc(s_ystore, 16)

            for i in range(NL):
                VE.wait(act, 0, ("x", i))
                if i:
                    AE.wait(act, 0, ("ss", i - 1))
                AE.done(nc.scalar.activation(sqj, x_sb[:, i], ACT.Square, accum_out=ss2[:, 16 + i:17 + i]), ("ss", i))
                VE.wait(act, 0, ("var", i))
                AE.done(nc.scalar.activation(ss2[:, 24 + i:25 + i], ss2[:, 20 + i:21 + i], ACT.Sqrt), ("sq", i))

        @block.vector
        def _(dve):
            n = [0]

            def mark(ins):
                n[0] += 1
                return ins.then_inc(s_fv, 1)

            def chain(ins):
                mark(ins)
                dve.wait_ge(s_fv, n[0])

            V = nc.vector

            def evac_front(i):
                dve.wait_ge(pc.full[i % 3], i // 3 + 1)
                s = 1 if i < NC else 0
                for k in range(4, KT):
                    ins = V.tensor_scalar(hT[:, k, i * P:(i + 1) * P], pc.banks[i % 3][:, (k - 4) * P:(k - 3) * P],
                                          ada_mod[:, k, s:s + 1], ada[:, k, s:s + 1], ALU.mult, ALU.add)
                ins.then_inc(pc.drained[i % 3], 1)

            dve.wait_ge(s_pool, 6)
            V.tensor_reduce(group_sum, ident[:].rearrange("p (g m) -> p m g", m=32), AX.X, ALU.add
                            ).then_inc(s_sum, 1)
            dve.wait_ge(s_fs, 6)
            mark(V.tensor_scalar(stat[:, 8:14], stat[:, 0:6], 1.0 / D, EPS, ALU.mult, ALU.add))
            dve.wait_ge(s_fs, 7)
            chain(V.reciprocal(stat[:, 16:22], stat[:, 8:14]))
            for i in range(C):
                src = ctx_sb[:, i] if i < NC else x_sb[:, i - NC]
                if i >= 2:
                    dve.wait_ge(pc.full[(i - 2) % 3], (i - 2) // 3 + 1)
                    dve.wait_ge(pb.full[i % 2], (i - 2) // 2 + 1)
                mark(V.tensor_scalar(xn[i % 2], src, stat[:, 16 + i:17 + i], None, ALU.mult))
                if i == 1:
                    dve.wait_ge(s_fps, 3)
                    dve.wait_ge(s_fs, 8)
                    chain(V.tensor_tensor(ada[:, 0:16, :], bank[0][:, 128:160].rearrange("p (a s) -> p a s", s=2),
                                          cols[:, 33:49].unsqueeze(2).to_broadcast([P, 16, 2]), ALU.add))
                    chain(V.scalar_tensor_tensor(ada_mod[:], ada[:, 8:16, :], 1.0,
                                                 cols[:, 16:24].unsqueeze(2).to_broadcast([P, 8, 2]),
                                                 ALU.add, ALU.mult))
                    assert n[0] == FV_MOD
                if i >= 1:
                    for j in ([0, 1] if i == 1 else [i]):
                        evac_front(j)
            for a in (pre_q[:, 0:2], pre_q[:, SEQ + 2:SEQ + 4], pre_k[:, 0:2], pre_k[:, CTX + 2:CTX + 6],
                      pre_k[:, CTX + SEQ + 6:CTX + SEQ + 8], pre_v[:, 0:2], pre_v[:, CTX + 2:CTX + 6],
                      pre_v[:, CTX + SEQ + 6:CTX + SEQ + 8]):
                ins = V.memset(a, 0.0)
            ins.then_inc(s_pads, 1)
            for part, (lo, n_tok) in enumerate(((0, 512), (512, 256))):
                dve.wait_ge(pb.full[2] if part else s_gfull, 1)
                V.tensor_copy(gate_rows[:, lo:lo + n_tok], bank[6 + part][:, 0:n_tok]).then_inc(
                    pb.drained[2] if part else s_gcopy, 1)
            dve.wait_ge(s_fps, 4)
            dve.wait_ge(s_small, 48)
            psg = bank[0][:, 192:384].rearrange("p (c n) -> p c n", c=C)
            mark(V.tensor_tensor(ga[0], psg[:, :, 0:16], rates[:, 16:32].unsqueeze(1).to_broadcast([P, C, 16]),
                                 ALU.add))
            assert n[0] == FV_U, n[0]
            mark(V.tensor_copy(ga[3], psg[:, :, 16:32]))
            assert n[0] == FV_GB
            dve.wait_ge(s_fs, 14)
            chain(V.scalar_tensor_tensor(ga[2], ga[0], 0.0, ga[1], ALU.max, ALU.add))
            dve.wait_ge(s_fs, 11)
            chain(V.scalar_tensor_tensor(ga[0], ga[2], -1.0, rates[:, 32:48].unsqueeze(1).to_broadcast([P, C, 16]),
                                         ALU.mult, ALU.mult))
            mark(V.tensor_copy(decays[:, 0:12, :].rearrange("p (d c) h -> p d c h", d=2),
                               ga[0].rearrange("p c (d h) -> p d c h", d=2)))
            assert n[0] == FV_G, n[0]
            dve.wait_ge(s_fs, 15)
            chain(V.tensor_scalar(decays[:, 60:72, :], decays[:, 24:36, :], -1.0, None, ALU.mult))
            dve.wait_ge(s_fs, 18)

            CONVS = {"q": (0, ("q",), pre_q, conv_q), "k": (1, ("k", "kc"), pre_k, conv_k), "v": (2, ("v", "vc"), pre_v, vT)}

            def taps(h):
                tapsig.done(V.tensor_copy(cw.unsqueeze(2), convc[:].rearrange("p (a h) -> p a h", h=H)[:, :, bass.ds(h, 1)]),
                            "cw")
                tapsig.done(V.tensor_copy(gc.rearrange("p d c -> p (d c)").unsqueeze(2), decays[:, 0:12, bass.ds(h, 1)]), "gc")

            def convolve(h, kind):
                s, tags, src, dst = CONVS[kind]
                width = dst.shape[1]
                for tag in tags:
                    pa.wait_drained(dve, h, tag)
                for k in range(CONV):
                    w = cw[:, k * 3 + s:k * 3 + s + 1]
                    if k == 0:
                        tapsig.wait(dve, h, "cw")
                        ins = V.tensor_scalar(dst, src[:, 0:width], w, None, ALU.mult)
                    else:
                        convd.wait(dve, h, (s, k - 1))
                        ins = V.scalar_tensor_tensor(dst, src[:, k:k + width], w, dst, ALU.mult, ALU.add)
                    convd.done(ins, (s, k))

            def head(h, more):
                colsig.done(V.tensor_copy(hc.rearrange("p q d c -> p (q d c)").unsqueeze(2),
                                          decays[:, :, bass.ds(h, 1)]), "hc")
                b = pc.wait_full(dve, h, "ss")
                pc.release(V.tensor_scalar(ssc, b[:, 0:10], EPS, None, ALU.add), "ss")
                pc.wait_drained(dve, h, "ss")
                small.done(V.reciprocal(r2, ssc[:, 0:6]), "r2")
                silu.wait(dve, h, "nrm")
                small.done(V.reciprocal(ofac[:, 20:24], nrm[:, 6:10]), "rq")
                small.wait(dve, h, "r2")
                small.done(V.tensor_tensor(c1, hc[:, 1], r2.unsqueeze(1).to_broadcast([P, 2, C]), ALU.mult), "c1")
                small.wait(dve, h, "c1")
                small.done(V.tensor_tensor(c3, c1, hc[:, 3], ALU.mult), "c3")
                for g in range(3):
                    b = pc.wait_full(dve, h, ("kq", g))
                    pb.wait_drained(dve, h, ("dt", g))
                    if g == 0:
                        small.wait(dve, h, "c1")
                    for u in range(4):
                        cc, d = 2 * g + u // 2, u % 2
                        ins = V.scalar_tensor_tensor(AT[g][:, u, :], b[:, (u // 2) * 256:(u // 2) * 256 + P],
                                                     c1[:, d, cc:cc + 1], gam[g][:, u, :], ALU.mult, ALU.mult)
                    if g == 0:
                        pc.release(ins, ("kq", g))
                        pc.wait_drained(dve, h, ("kq", g))
                    else:
                        atd.done(ins, g)
                        atd.wait(dve, h, g)
                    lm0.done(V.tensor_tensor(Lm[g][0].rearrange("p (c d) i -> p c d i", d=2),
                                             AT[g].rearrange("p (c d) i -> p c d i", d=2),
                                             lvl[:, 0:1, :, :].to_broadcast([P, 2, 2, P]), ALU.mult), g)
                    if g:
                        gammask.wait(dve, h, g)
                        for e in range(2):
                            ins = V.tensor_tensor(
                                PT[g - 1][:, 2 * e:2 * e + 2, :],
                                b[:, e * 256 + P:e * 256 + 2 * P].unsqueeze(1).to_broadcast([P, 2, P]),
                                gamI[g - 1][:, 2 * e:2 * e + 2, :], ALU.mult)
                        pc.release(ins, ("kq", g))
                for g in range(3):
                    b = pc.wait_full(dve, h, ("lt", g))
                    pc.release(V.tensor_tensor(T[g], ident[:].unsqueeze(1).to_broadcast([P, 4, P]),
                                               b[:].rearrange("p (u i) -> p u i", u=4), ALU.subtract), ("lt", g))
                for l, g in items:
                    b = pc.wait_full(dve, h, ("X", l, g))
                    if l == 1:
                        x0.wait(dve, h, g)
                    pc.release(V.tensor_tensor(X[g], X[g], b[:].rearrange("p (u i) -> p u i", u=4), ALU.subtract),
                               ("X", l, g))
                for t in range(C):
                    unit = [(d, ORDER[d][t]) for d in range(2)]
                    if t:
                        b = pc.wait_full(dve, h, ("ks", t))
                        for d, cc in unit:
                            ins = V.scalar_tensor_tensor(R[:, d], b[:, d * P:(d + 1) * P], hc[:, 5, d, cc:cc + 1],
                                                         Vn[:, cc], ALU.mult, ALU.add)
                        if t < NC:
                            pc.release(ins, ("ks", t))
                        else:
                            scan.done(ins, ("R", t))
                        if more and t == 1:
                            taps(h + 1)
                        if more and t in (3, 5):
                            convolve(h + 1, {3: "k", 5: "v"}[t])
                    else:
                        pb.wait_drained(dve, h, "vt")
                    y = pc.wait_full(dve, h, ("y", t))
                    if t == 0:
                        small.wait(dve, h, "c3")
                    for d, cc in unit:
                        ins = V.tensor_scalar(vS[:, d], y[:, d * P:(d + 1) * P], c3[:, d, cc:cc + 1], None, ALU.mult)
                    if t >= NC:
                        scan.done(ins, ("vS", t))
                        for d, cc in unit:
                            ins = V.tensor_scalar(vP[:, d], y[:, d * P:(d + 1) * P], c1[:, d, cc:cc + 1], None, ALU.mult)
                    pc.release(ins, ("y", t))
                    if t < C - 1:
                        b = pc.wait_full(dve, h, ("su", t))
                        for d, cc in unit:
                            if t == 0:
                                ins = V.tensor_copy(S[:, d], b[:, d * P:(d + 1) * P])
                            else:
                                ins = V.scalar_tensor_tensor(S[:, d], S[:, d], hc[:, 4, d, cc:cc + 1],
                                                             b[:, d * P:(d + 1) * P], ALU.mult, ALU.add)
                        pc.release(ins, ("su", t))
                    if t >= NC:
                        b = pc.bank(("ks", t))
                        for d, cc in unit:
                            src, col = b[:, 256 + d * P:384 + d * P], hc[:, 2, d, cc:cc + 1]
                            if ORDER[1 - d].index(cc) > t:
                                ins = V.tensor_scalar(oacc[:, cc - NC], src, col, None, ALU.mult)
                            else:
                                pc.wait_drained(dve, h, ("o", t - 1))
                                ins = V.scalar_tensor_tensor(oacc[:, cc - NC], src, col, oacc[:, cc - NC],
                                                             ALU.mult, ALU.add)
                        pc.release(ins, ("ks", t))
                        b = pc.wait_full(dve, h, ("o", t))
                        pc.wait_drained(dve, h, ("ks", t))
                        for d, cc in unit:
                            ins = V.tensor_tensor(oacc[:, cc - NC], oacc[:, cc - NC], b[:, d * P:(d + 1) * P], ALU.add)
                        pc.release(ins, ("o", t))
                post.done(V.tensor_scalar(ofac[:, 4:8], ofac[:, 20:24], float(P) ** -0.5, None, ALU.mult), "a")
                post.wait(dve, h, "a")
                post.done(V.tensor_tensor(ofac[:, 8:12], ofac[:, 4:8], ofac[:, 4:8], ALU.mult), "a2")
                postA.wait(dve, h, "ss")
                post.wait(dve, h, "a2")
                post.done(V.tensor_tensor(ofac[:, 16:20], ofac[:, 8:12], ofac[:, 0:4], ALU.mult), "m")
                post.wait(dve, h, "m")
                post.done(V.tensor_scalar(ofac[:, 8:12], ofac[:, 16:20], 1.0 / P, EPS, ALU.mult, ALU.add), "var")
                postA.wait(dve, h, "sqrt")
                post.done(V.reciprocal(ofac[:, 16:20], ofac[:, 12:16]), "rstd")
                post.wait(dve, h, "rstd")
                post.done(V.tensor_tensor(ofac[:, 12:16], ofac[:, 16:20], ofac[:, 4:8], ALU.mult), "fac")
                post.wait(dve, h, "fac")
                for i in range(NL):
                    ins = V.scalar_tensor_tensor(on[:, i], oacc[:, i], ofac[:, 12 + i:13 + i], zs[:, i], ALU.mult, ALU.mult)
                post.done(ins, "on")
                if more:
                    convolve(h + 1, "q")

            taps(0)
            for kind in "kvq":
                convolve(0, kind)
            with dve.Fori(0, H - 1) as h:
                head(h, True)
            head(H - 1, False)

            def wait(*tags):
                for t in tags:
                    VT.wait(dve, 0, t)

            bc = lambda a, shape: a.to_broadcast(shape)
            pb.wait_drained(dve, H - 1, "ada3")
            VT.done(V.tensor_tensor(ada[:, 16:48, :], ada[:, 16:48, :], bc(cols[:, 49:81].unsqueeze(2), [P, 32, 2]),
                                    ALU.add), "ada2")
            wait("ada2")
            VT.done(V.scalar_tensor_tensor(ada_mod[:], ada[:, 32:40, :], 1.0,
                                           bc(cols[:, 24:32].unsqueeze(2), [P, 8, 2]), ALU.add, ALU.mult), "A2")
            for n, (first, dst) in enumerate(((16, g1b), (40, g2b))):
                if n:
                    PT_.wait(dve, 0, "g1")
                for k in range(KT):
                    ins = V.tensor_scalar(diag[:, k, :], ident[:], ada[:, first + k, 0:1], None, ALU.mult)
                VT.done(ins, ("dg1", "dg2")[n])
                PT_.wait(dve, 0, ("g1", "g2")[n])
                for j in range(2):
                    ins = V.tensor_copy(dst[:, j * 512:(j + 1) * 512], bank[2 * n + j][:])
                VT.done(ins, ("g1b", "g2b")[n])

            def norm2(i):
                AT_.wait(dve, 0, ("ss", i))
                VT.done(V.tensor_scalar(ss2[:, 4 + i:5 + i], ss2[:, i:i + 1], 1.0 / D, EPS, ALU.mult, ALU.add), ("var", i))
                AT_.wait(dve, 0, ("sq", i))
                VT.done(V.reciprocal(ss2[:, 12 + i:13 + i], ss2[:, 8 + i:9 + i]), ("rs", i))
                wait(("rs", i))
                if i >= 2:
                    PT_.wait(dve, 0, ("tr", i - 2))
                    dve.wait_ge(s_store[i - 2], 16)
                VT.done(V.tensor_scalar(xn2[i % 2], x_sb[:, i], ss2[:, 12 + i:13 + i], None, ALU.mult), ("xn", i))

            for i in range(NL):
                PT_.wait(dve, 0, ("wo", i))
                wait("g1b", ("x", i - 1) if i else "g2b")
                for j in range(2):
                    ins = V.tensor_tensor(tmp[:, j * 512:(j + 1) * 512], bank[4 + (2 * i + j) % 4][:],
                                          g1b[:, j * 512:(j + 1) * 512], ALU.mult)
                VT.done(ins, ("m", i))
                wait(("m", i))
                VT.done(V.tensor_tensor(x_sb[:, i], x_sb[:, i], tmp, ALU.add), ("x", i))
                if i:
                    norm2(i - 1)
            norm2(NL - 1)
            dve.wait_ge(s_rw, 32)
            for i in range(NL):
                PT_.wait(dve, 0, ("lo", i))
                VT.done(V.tensor_tensor(lg[:, i], bank[4][:, 32 * i:32 * i + 32], rb, ALU.add), ("lg", i))
                wait(("lg", i))
                VT.done(V.max(top[:, i], lg[:, i]), ("top", i))
                wait(("top", i))
                VT.done(V.max_index(topi[:, i], top[:, i], lg[:, i]), ("topi", i))
            wait(("topi", 3))
            VT.done(V.tensor_copy(topf, topi[:, :, 0:TOPK]), "topf")
            VT.done(V.tensor_tensor(ex, top[:, :, 0:TOPK], bc(top[:, :, 0:1], [P, NL, TOPK]), ALU.subtract), "sub")
            wait("topf")
            dve.wait_ge(s_iota, 3)
            VT.done(V.tensor_tensor(OE.rearrange("p i k e -> p (i k) e"), bc(iota64[:, 0:E].unsqueeze(1), [P, 16, E]),
                                    bc(topf.rearrange("p i k -> p (i k)").unsqueeze(2), [P, 16, E]), ALU.is_equal), "OE")
            wait("OE")
            VT.done(V.tensor_reduce(M, OE.rearrange("p i k e -> p i e k"), AX.X, ALU.add), "M")
            AT_.wait(dve, 0, "exp")
            VT.done(V.tensor_reduce(exs[:, 0:NL], ex, AX.X, ALU.add), "sum")
            wait("sum")
            VT.done(V.reciprocal(exs[:, NL:2 * NL], exs[:, 0:NL]), "rec")
            wait("rec")
            VT.done(V.tensor_tensor(gates[:], ex, bc(exs[:, NL:2 * NL].unsqueeze(2), [P, NL, TOPK]), ALU.mult), "gates")
            PT_.wait(dve, 0, "pos")
            VT.done(V.tensor_copy(cnt, bank[5][:, 128:160]), ("nb", 0))
            wait(("nb", 0))
            for j in range(1, 8):
                if j == 1:
                    ins = V.tensor_scalar(nbf, cnt, float(BLK), 1.0, ALU.is_gt, ALU.add)
                else:
                    wait(("nb", j - 1))
                    ins = V.scalar_tensor_tensor(nbf, cnt, float(BLK * j), nbf, ALU.is_gt, ALU.add)
                VT.done(ins, ("nb", j))
            wait(("nb", 7))
            VT.done(V.tensor_tensor_scan(cnt, ones[:, 0:E], nbf, 0.0, ALU.mult, ALU.add), "bsi")
            wait("bsi")
            VT.done(V.tensor_tensor(bsf, cnt, nbf, ALU.subtract), "bs")
            wait("bs")
            V.tensor_copy(plan[0:1, 0:E], nbf[0:1, :])
            V.tensor_copy(plan[0:1, 3 * E:3 * E + 1], cnt[0:1, E - 1:E])
            V.tensor_scalar(plan[0:1, 2 * E:3 * E], cnt[0:1, :], 1.0, None, ALU.subtract)
            VT.done(V.tensor_copy(plan[0:1, E:2 * E], bsf[0:1, :]), "plan")
            VT.done(V.scalar_tensor_tensor(slot_of, bc(bsf.unsqueeze(1), [P, NL, E]), float(BLK),
                                           bank[5][:, 0:128].rearrange("p (i e) -> p i e", i=NL), ALU.mult, ALU.add), "dst")
            wait("dst")
            VT.done(V.tensor_tensor(prod, OE, bc(slot_of.unsqueeze(2), [P, NL, TOPK, E]), ALU.mult), "prod")
            wait("prod")
            VT.done(V.tensor_reduce(dest, prod.rearrange("p i k e -> p (i k) e"), AX.X, ALU.add), "dest")
            wait("dest")
            VT.done(V.tensor_copy(yrow_of[:], dest), "yrow")
            VT.done(V.tensor_copy(desti, dest), "desti")
            wait("desti")
            VT.done(V.tensor_scalar(blki, desti, 6, None, ALU.logical_shift_right), "blki")
            VT.done(V.tensor_scalar(sloti, desti, BLK - 1, None, ALU.bitwise_and), "sloti")
            wait("sloti")
            VT.done(V.tensor_copy(blkf, blki), "blkf")
            VT.done(V.tensor_copy(slotf, sloti), "slotf")
            wait("slotf")
            n16 = [P, 16, BLK]
            VT.done(V.tensor_tensor(OS, bc(iota64.unsqueeze(1), n16), bc(slotf.unsqueeze(2), n16), ALU.is_equal), "OS")
            VT.done(V.tensor_tensor(OB, bc(iota64.unsqueeze(1), n16), bc(blkf.unsqueeze(2), n16), ALU.is_equal), "OB")
            wait("OB")
            OBf = OB.rearrange("p (i k) s -> p i (k s)", i=NL)
            VT.done(V.tensor_tensor(OBf, OBf, bc(tokid.unsqueeze(2), [P, NL, TOPK * BLK]), ALU.mult), "OBt")
            PT_.wait(dve, 0, "ids")
            VT.done(V.tensor_copy(tok_of[:, 0:BLK], bank[6][0:BLK, 0:BLK]), "tok_of")

            d8 = [P, 8, BLK]
            ps8 = lambda b: bank[b][:].rearrange("p (f t) -> p f t", f=8)

            dve.wait_ge(PEs.sem, 1)
            V.tensor_tensor(xT, ps8(3), bc(ada_mod[:, :, 0:1], d8), ALU.mult).then_inc(DVs.sem, 1)
            dve.wait_ge(DVs.sem, 1)
            V.tensor_tensor(xT, xT, bc(ada[:, 24:32, 0:1], d8), ALU.add).then_inc(DVs.sem, 1)

            with dve.Fori(0, E) as e:
                nb = dve.value_load(plan[0:1, bass.ds(e, 1)], min_val=1, max_val=SEQ // BLK)
                bs = dve.value_load(plan[0:1, bass.ds(e + E, 1)], min_val=0, max_val=NBLK)
                dve.wait_ge(PEs.sem, bs * len(PEs.tags) + 1)
                V.tensor_copy(pick_now[:], bc(pick[:, bass.ds(e, 1)], [3 * E, BLK])).then_inc(s_pick, 1)
                with dve.Fori(0, nb) as i:
                    b = bs + i
                    PEs.wait(dve, b, "g")
                    DVs.done(V.tensor_scalar(glu, bank[0][:], 7.0, None, ALU.min), "glu")
                    ACs.wait(dve, b, "sig")
                    DVs.done(V.tensor_tensor(sig, glu, sig, ALU.mult), "m")
                    for j in range(2):
                        f = slice(256 * j, 256 * j + 256)
                        PEs.wait(dve, b, f"l{j}")
                        DVs.done(V.tensor_scalar(lin[:, f], bank[(1, 6)[j]][:, 0:256], 7.0, -7.0, ALU.min, ALU.max), f"c{j}")
                        DVs.wait(dve, b, f"c{j}")
                        DVs.done(V.scalar_tensor_tensor(act_rows[:, f], lin[:, f], 1.0, sig[:, f], ALU.add, ALU.mult),
                                 f"act{j}")
                    PEs.wait(dve, b, "xt")
                    DVs.done(V.tensor_tensor(xT, ps8(3), bc(ada_mod[:, :, 0:1], d8), ALU.mult), "xa")
                    DVs.wait(dve, b, "xa")
                    DVs.done(V.tensor_tensor(xT, xT, bc(ada[:, 24:32, 0:1], d8), ALU.add), "xb")

            def ew(*tags):
                for t in tags:
                    VE.wait(dve, 0, t)

            def last_norm(i):
                AE.wait(dve, 0, ("ss", i))
                VE.done(V.tensor_scalar(ss2[:, 20 + i:21 + i], ss2[:, 16 + i:17 + i], 1.0 / D, EPS, ALU.mult, ALU.add),
                        ("var", i))
                AE.wait(dve, 0, ("sq", i))
                VE.done(V.reciprocal(ss2[:, 28 + i:29 + i], ss2[:, 24 + i:25 + i]), ("rs", i))
                ew(("rs", i))
                VE.done(V.scalar_tensor_tensor(ofin[i], x_sb[:, i], ss2[:, 28 + i:29 + i], fg, ALU.mult, ALU.mult),
                        ("out", i))

            dve.wait_ge(s_fg, 16)
            for i in range(NL):
                for k in range(TOPK):
                    dve.wait_ge(s_back[TOPK * i + k], 16)
                    src, gate_k = got[TOPK * i + k], gates[:, i, k:k + 1]
                    if k == 0:
                        ins = V.tensor_scalar(osum[i], src, gate_k, None, ALU.mult)
                    else:
                        ew(("c", i, k - 1))
                        ins = V.scalar_tensor_tensor(osum[i], src, gate_k, osum[i], ALU.mult, ALU.add)
                    VE.done(ins, ("c", i, k))
                ew(("c", i, TOPK - 1))
                VE.done(V.tensor_tensor(osum[i], osum[i], g2b, ALU.mult), ("g", i))
                ew(("g", i))
                VE.done(V.tensor_tensor(x_sb[:, i], x_sb[:, i], osum[i], ALU.add), ("x", i))
                if i:
                    last_norm(i - 1)
            last_norm(NL - 1)

        @block.tensor
        def _(pe):
            mm = nc.tensor.matmul
            tr = nc.tensor.transpose
            step = [0]

            def fstep(ins):
                step[0] += 1
                ins.then_inc(s_fps, 1)

            def modulation_rows(out_bank, w):
                for k in range(KT):
                    g = slice(32 * (k % 4), 32 * (k % 4) + 32)
                    ins = mm(out_bank[g, :], sc[:, k, :], w[:, k, :], start=(k < 4), stop=(k >= 4))
                return ins

            pe.wait_ge(s_pool, 6)
            pe.wait_ge(s_rows, 96)
            fstep(tr(bank[0][:, 0:81], rows[0:81, 0:P], ident[0:81, 0:81]))
            pe.wait_ge(s_small, 48)
            fstep(tr(bank[1][:, 0:120], rows[0:120, P:2 * P], ident[0:120, 0:120]))
            pe.wait_ge(s_fs, 9)
            for i in range(4):
                pe.wait_ge(s_adaw[i], 16)
                modulation_rows(bank[4 + i], first_ada[i]).then_inc(s_rfull, 1)
            pe.wait_ge(s_sum, 1)
            for i in range(4):
                pe.wait_ge(s_rcopy, i + 1)
                for a in range(4):
                    ins = mm(bank[0][:, 128 + 8 * i + 2 * a:130 + 8 * i + 2 * a], first_rows[i][:, a * P:(a + 1) * P],
                             group_sum[:, 0:2], start=True, stop=True)
            fstep(ins)
            for i in range(C):
                pe.wait_ge(s_fv, 3 + i if i < 2 else FV_MOD + i - 1)
                if i >= 2:
                    pe.wait_ge(pb.drained[i % 2], (i - 2) // 2 + 1)
                if i >= 3:
                    pe.wait_ge(pc.drained[i % 3], 1)
                for k in range(KT):
                    b = pb.banks[i % 2] if k < 4 else pc.banks[i % 3]
                    ins = tr(b[:, (k % 4) * P:(k % 4 + 1) * P], xn[i % 2][:, k * P:(k + 1) * P], ident[:])
                    if k == 3:
                        ins.then_inc(pb.full[i % 2], 1)
                ins.then_inc(pc.full[i % 3], 1)
            pe.wait_ge(s_wgate, 16)
            for i in range(C):
                pe.wait_ge(pb.drained[i % 2], i // 2 + 1)
                pe.wait_ge(pc.drained[i % 3], i // 3 + 1)
            for part, (lo, n_tok) in enumerate(((0, 512), (512, 256))):
                for k in range(KT):
                    g = slice(32 * (k % 4), 32 * (k % 4) + 32)
                    ins = mm(bank[6 + part][g, 0:n_tok], wgate[:, k, :], hT[:, k, lo:lo + n_tok], start=(k < 4), stop=(k >= 4))
                ins.then_inc(pb.full[2] if part else s_gfull, 1)
            for i in range(C):
                pe.wait_ge(pb.drained[2] if i // 4 else s_gcopy, 1)
                ins = mm(bank[0][:, 192 + 32 * i:224 + 32 * i], gate_rows[:, i * P:(i + 1) * P], group_sum,
                         start=True, stop=True)
            fstep(ins)
            pe.wait_ge(s_fv, FV_G)
            pe.wait_ge(s_pool, 10)
            for j, (mf, mb) in enumerate(((tri[:, LE], tri[:, GE]), (tri[:, GT], tri[:, LT]), (ones[:], ones[:]))):
                for d, m in enumerate((mf, mb)):
                    ins = mm(bank[1][:, 96 * j + 48 * d:96 * j + 48 * d + 48], m,
                             decays[:, 6 * d:6 * d + 6, :], start=True, stop=True)
            fstep(ins)
            pe.wait_ge(s_fs, 18)
            pe.wait_ge(s_pads, 1)

            def project(h, tag):
                q = {"q": 0, "k": 1, "v": 2, "kc": 1, "vc": 2}[tag]
                lo, n_tok = (0, CTX) if tag in ("kc", "vc") else (CTX, SEQ)
                if tag in "qkv":
                    pe.wait_ge(win_loaded[q], 16 * h + 16)
                b = pa.open(pe, h, tag)
                for k in range(KT):
                    ins = mm(b[:, 0:n_tok], win[:, q, k, :], hT[:, k, lo:lo + n_tok], start=(k == 0), stop=(k == KT - 1))
                pa.close(ins, tag)

            def project_z(h):
                pe.wait_ge(win_loaded[3], 16 * h + 16)
                b = pa.open(pe, h, "z")
                for i in range(NL):
                    for k in range(KT):
                        ins = mm(b[:, i * P:(i + 1) * P], hT[:, k, CTX + i * P:CTX + (i + 1) * P], win[:, 3, k, :],
                                 start=(k == 0), stop=(k == KT - 1))
                pa.close(ins, "z")

            def head(h, more):
                silu.wait(pe, h, "v")
                chunks = [(kT, i) for i in range(C)] + [(vT, i) for i in range(C)]
                for n, tag in enumerate(("kt0", "kt1", "vt")):
                    b = pb.open(pe, h, tag)
                    for j, (src, i) in enumerate(chunks[4 * n:4 * n + 4]):
                        ins = tr(b[:, j * P:(j + 1) * P], src[:, tcol(i):tcol(i) + P], ident[:])
                    pb.close(ins, tag)
                silu.wait(pe, h, "sqq")
                b = pc.open(pe, h, "ss")
                for i in range(10):
                    src = sq_k[:, tcol(i):tcol(i) + P] if i < C else sq_q[:, (i - C) * P:(i - C + 1) * P]
                    ins = mm(b[:, i:i + 1], src, ones[:, 0:1], start=True, stop=True)
                pc.close(ins, "ss")
                for g in range(3):
                    b = pc.open(pe, h, ("kq", g))
                    for e in range(2):
                        cc = 2 * g + e
                        key = kT[:, tcol(cc):tcol(cc) + P]
                        ins = mm(b[:, e * 256:e * 256 + P], key, key, start=True, stop=True)
                        if g:
                            ins = mm(b[:, e * 256 + P:e * 256 + 2 * P], key, qT[:, (cc - NC) * P:(cc - NC + 1) * P],
                                     start=True, stop=True)
                    pc.close(ins, ("kq", g))
                    (GUlast if g == 2 else GUd).wait(pe, h, g)
                    b = pb.open(pe, h, ("dt", g))
                    for u in range(4):
                        ins = mm(b[:, u * P:(u + 1) * P], tri[:, LT if u % 2 else GT], GU[g % 2][:, u, :],
                                 start=True, stop=True)
                    pb.close(ins, ("dt", g))
                for g in range(3):
                    lm0.wait(pe, h, g)
                    b = pc.open(pe, h, ("lt", g))
                    for u in range(4):
                        ins = tr(b[:, u * P:(u + 1) * P], Lm[g][0][:, u, :], ident[:])
                    pc.close(ins, ("lt", g))

                def mul_p(l, g):
                    lmsig.wait(pe, h, (l, g))
                    if l == 1:
                        pc.wait_drained(pe, h, ("lt", g))
                    else:
                        pb.wait_drained(pe, h, ("T", l - 1, g))
                    b = pb.open(pe, h, ("P", l, g))
                    for u in range(4):
                        ins = mm(b[:, u * P:(u + 1) * P], Lm[g][l % 2][:, u, :], T[g][:, u, :], start=True, stop=True)
                    pb.close(ins, ("P", l, g))

                def mul_x(l, g):
                    pb.wait_drained(pe, h, ("P", l, g))
                    if l == 1:
                        x0.wait(pe, h, g)
                    b = pc.open(pe, h, ("X", l, g))
                    for u in range(4):
                        ins = mm(b[:, u * P:(u + 1) * P], Pb[g][:, u, :], X[g][:, u, :], start=True, stop=True)
                    pc.close(ins, ("X", l, g))

                def turn(l, g):
                    pc.wait_drained(pe, h, ("X", l, g))
                    b = pb.open(pe, h, ("T", l, g))
                    for u in range(4):
                        ins = tr(b[:, u * P:(u + 1) * P], X[g][:, u, :], ident[:])
                    pb.close(ins, ("T", l, g))

                mul_p(*items[0])
                mul_p(*items[1])
                for n, item in enumerate(items):
                    if n and items[n - 1][0] < len(LEVELS) - 1:
                        turn(*items[n - 1])
                    mul_x(*item)
                    if n + 2 < len(items):
                        mul_p(*items[n + 2])

                def modulation():
                    pe.wait_ge(ada_loaded, 16 * h + 16)
                    pb.close(modulation_rows(pb.open(pe, h, "adar"), adaw), "adar")

                def modulation_columns():
                    pb.wait_drained(pe, h, "adar")
                    for n in range(4):
                        b = pb.open(pe, h, f"ada{n}")
                        pb.close(mm(b[:, 0:2], ada_rows[:, n * P:(n + 1) * P], group_sum[:, 0:2], start=True, stop=True),
                                 f"ada{n}")

                fill = [[modulation], [], [modulation_columns], [], [], []]
                if more:
                    for at, tag in enumerate(("k", "kc", "v", "vc", "q")):
                        fill[at + 1].insert(0, lambda tag=tag: project(h + 1, tag))
                unit = lambda d, cc: X[cc // 2][:, 2 * (cc % 2) + d, :]
                punit = lambda d, cc: PT[cc // 2 - 1][:, 2 * (cc % 2) + d, :]
                for t in range(C):
                    if t:
                        pc.wait_drained(pe, h, ("su", t - 1))
                        b = pc.open(pe, h, ("ks", t))
                        for d in range(2):
                            cc = ORDER[d][t]
                            ins = mm(b[:, d * P:(d + 1) * P], kT[:, tcol(cc):tcol(cc) + P], S[:, d], start=True, stop=True)
                        if t >= NC:
                            for d in range(2):
                                cc = ORDER[d][t]
                                ins = mm(b[:, 256 + d * P:384 + d * P], qT[:, (cc - NC) * P:(cc - NC + 1) * P], S[:, d],
                                         start=True, stop=True)
                        pc.close(ins, ("ks", t))
                    else:
                        for g in range(3):
                            pc.wait_drained(pe, h, ("X", 6, g))
                    for work in fill[t]:
                        work()
                    b = pc.open(pe, h, ("y", t))
                    for d in range(2):
                        cc = ORDER[d][t]
                        if t:
                            scan.wait(pe, h, ("R", t)) if t >= NC else pc.wait_drained(pe, h, ("ks", t))
                        else:
                            pb.wait_drained(pe, h, "kt1")
                        ins = mm(b[:, d * P:(d + 1) * P], unit(d, cc), R[:, d] if t else Vn[:, cc], start=True, stop=True)
                    pc.close(ins, ("y", t))
                    if t < C - 1:
                        b = pc.open(pe, h, ("su", t))
                        for d in range(2):
                            cc = ORDER[d][t]
                            scan.wait(pe, h, ("vS", t)) if t >= NC else pc.wait_drained(pe, h, ("y", t))
                            ins = mm(b[:, d * P:(d + 1) * P], Kn[:, cc], vS[:, d], start=True, stop=True)
                        pc.close(ins, ("su", t))
                    if t >= NC:
                        pc.wait_drained(pe, h, ("y", t))
                        b = pc.open(pe, h, ("o", t))
                        for d in range(2):
                            cc = ORDER[d][t]
                            ins = mm(b[:, d * P:(d + 1) * P], punit(d, cc), vP[:, d], start=True, stop=True)
                        pc.close(ins, ("o", t))
                if more:
                    project_z(h + 1)
                post.wait(pe, h, "on")
                b = pb.open(pe, h, "ot")
                for i in range(NL):
                    ins = tr(b[:, i * P:(i + 1) * P], on[:, i], ident[:])
                pb.close(ins, "ot")

            for tag in ("k", "kc", "v", "vc", "q"):
                project(0, tag)
            project_z(0)
            with pe.Fori(0, H - 1) as h:
                head(h, True)
            head(H - 1, False)

            for n in range(2):
                VT.wait(pe, 0, ("dg1", "dg2")[n])
                if n == 0:
                    pa.wait_drained(pe, H - 1, "z")
                else:
                    pb.wait_drained(pe, H - 1, "ot")
                for k in range(KT):
                    ins = mm(bank[2 * n + k // 4][:, (k % 4) * P:(k % 4 + 1) * P], ones[:], diag[:, k, :],
                             start=True, stop=True)
                PT_.done(ins, ("g1", "g2")[n])

            def out_proj(i):
                if i < 2:
                    pc.wait_drained(pe, H - 1, scan_tags[-1])
                else:
                    VT.wait(pe, 0, ("m", i - 2))
                for j in range(2):
                    for h in range(H):
                        ins = mm(bank[4 + (2 * i + j) % 4][:], oT[:, h, i * P:(i + 1) * P], wout[:, h, j * 512:(j + 1) * 512],
                                 start=(h == 0), stop=(h == H - 1))
                PT_.done(ins, ("wo", i))

            def turn(i):
                VT.wait(pe, 0, ("xn", i))
                if i >= 2:
                    AT_.wait(pe, 0, ("h2T", i - 2))
                for k in range(KT):
                    ins = tr(bank[(2 * i + k // 4) % 4][:, (k % 4) * P:(k % 4 + 1) * P], xn2[i % 2][:, k * P:(k + 1) * P],
                             ident[:])
                PT_.done(ins, ("tr", i))

            def logits(i):
                AT_.wait(pe, 0, ("h2T", i))
                VT.wait(pe, 0, ("lg", i - 1) if i else ("m", 2))
                for k in range(KT):
                    ins = mm(bank[4][:, 32 * i:32 * i + 32], h2T[:, k, :], rw[:, k, :], start=(k == 0), stop=(k == KT - 1))
                PT_.done(ins, ("lo", i))

            pe.wait_ge(s_wout, 16)
            pe.wait_ge(s_rw, 32)
            pb.wait_drained(pe, H - 1, "ot")
            for kind, i in (a for a in pe_tags if isinstance(a, tuple)):
                {"wo": out_proj, "tr": turn, "lo": logits}[kind](i)
            VT.wait(pe, 0, "M")
            for i in range(NL):
                for j in range(i + 1):
                    mm(bank[5][:, 32 * i:32 * i + 32], ones[:] if j < i else tri[:, LT], M[:, j], start=(j == 0), stop=(j == i))
            for j in range(NL):
                ins = mm(bank[5][:, 128:160], ones[:], M[:, j], start=(j == 0), stop=(j == NL - 1))
            PT_.done(ins, "pos")
            VT.wait(pe, 0, "OBt")
            for j in range(NL * TOPK):
                ins = mm(bank[6][0:BLK, 0:BLK], OS[:, j, :], OB[:, j, :], start=(j == 0), stop=(j == NL * TOPK - 1))
            PT_.done(ins, "ids")

            def turn_x():
                for k in range(KT):
                    ins = tr(bank[3][:, k * BLK:(k + 1) * BLK], xg[:, k * P:(k + 1) * P], ident[0:BLK, 0:BLK])
                return ins

            pe.wait_ge(s_gather, 16)
            turn_x().then_inc(PEs.sem, 1)

            with pe.Fori(0, E // 4) as it:
                for j in range(4):
                    e = 4 * it + j
                    nb = pe.value_load(plan[0:1, bass.ds(e, 1)], min_val=1, max_val=SEQ // BLK)
                    bs = pe.value_load(plan[0:1, bass.ds(e + E, 1)], min_val=0, max_val=NBLK)
                    with pe.Fori(0, nb) as i:
                        b = bs + i
                        def pair(out_bank, m, lhs, col, cols_of=slice(0, 512), order=range(KT), between=None, then=None):
                            lo, hi = cols_of.start, cols_of.stop
                            for q in (m, m + 1):
                                pe.wait_ge(slot_loaded[q % NSLOT], 16 * (3 * it + q // NSLOT + 1))
                            for n, k in enumerate(order):
                                if between and n in between:
                                    between[n]()
                                for q in range(2):
                                    mm(out_bank[q * BLK:(q + 1) * BLK, 0:hi - lo], lhs(k), slots[(m + q) % NSLOT][:, k, lo:hi],
                                       start=(n == 0), stop=False)
                            pe.wait_ge(s_pick, e + 1)
                            if then is not None:
                                pe.wait_ge(s_gather, then)
                            for q in range(2):
                                ins = mm(out_bank[q * BLK:(q + 1) * BLK, 0:hi - lo], pick_now[:],
                                         bias[:, col + q * 512 + lo:col + q * 512 + hi], start=False, stop=True)
                            return ins

                        def turn_act(a):
                            DVs.wait(pe, b, f"act{a}")
                            for n in range(2):
                                ins = tr(bank[4 + a][:, n * P:(n + 1) * P],
                                         act_rows[:, (2 * a + n) * P:(2 * a + n + 1) * P], ident[:])
                            PEs.done(ins, f"at{a}")

                        token = lambda k: xT[:, k, :]
                        pe.wait_ge(DVs.sem, b * len(DVs.tags) + 2)
                        PEs.done(pair(bank[0], 6 * j, token, 0), "g")
                        PEs.done(pair(bank[1], 6 * j + 2, token, FF, slice(0, 256)), "l0")
                        PEs.done(pair(bank[6], 6 * j + 2, token, FF, slice(256, 512), then=16 * b + 32), "l1")
                        PEs.done(turn_x(), "xt")
                        turn_act(0)
                        ACs.wait(pe, b, "at0")
                        PEs.done(pair(bank[2], 6 * j + 4, lambda k: act_T[:, k % 4, k // 4, :], 2 * FF,
                                      order=(0, 1, 4, 5, 2, 3, 6, 7),
                                      between={2: lambda: turn_act(1), 4: lambda: ACs.wait(pe, b, "at1")}), "d")


INPUTS = ["x", "c", "ctx", "c_ctx", "ada_w", "ada_b", "norm_mix_g", "norm_ffn_g", "final_g", "gdn_w_in", "gdn_conv_w",
          "gdn_a_log", "gdn_dt_bias", "gdn_norm_g", "gdn_w_out", "router_w", "router_b", "moe_w_gu", "moe_b_gu",
          "moe_w_down", "moe_b_down"]


def kernel(**inputs):
    import numpy as np
    import concourse.bacc as bacc
    from concourse.bass_utils import run_bass_kernel_spmd as run

    nc = bacc.Bacc("TRN2", target_bir_lowering=False, num_devices=1)
    arrays, args = {}, []
    for name in INPUTS:
        a = np.ascontiguousarray(inputs[name])
        arrays[f"in_{name}"] = a
        args.append(nc.dram_tensor(f"in_{name}", a.shape, mybir.dt.from_np(a.dtype), kind="ExternalInput").ap())
    out = nc.dram_tensor("out", (1, SEQ, D), F32, kind="ExternalOutput").ap()
    trunk(nc, *args, out)
    return run(nc, [arrays], core_ids=[0]).results[0]["out"]
```
